# Optimizing a Trainium2 kernel written in Bass

```python
import math
import jax, jax.numpy as jnp
from jax import lax
import numpy as np

D_MODEL = 1024
BATCH = 1
SEQ = 256
DEPTH = 2

GRID_W = 64
CTX_LEN = 256
N_EVEN = (DEPTH + 1) // 2
N_ODD = DEPTH // 2
RMS_EPS = 1e-6
N_MOD = 6

A_HEADS = 4
A_DQK = 64
A_DV = 128
Q_BLOCK = 128
ROPE_BASE = 10000.0
ROPE_AXIS_PAIRS = A_DQK // 4

B_HEADS = 4
B_DH = 128
B_WIDTH = B_HEADS * B_DH
CHUNK = 64
SHORT_CONV = 3

A_QW = A_HEADS * 2 * A_DQK
A_VW = A_HEADS * A_DV
GATE_W = 4 * B_HEADS
Q_SIDE = A_QW + 2 * B_WIDTH
KV_SIDE = A_QW + A_VW + 2 * B_WIDTH + GATE_W
P_AB = Q_SIDE + KV_SIDE
MIX_W = A_VW + B_WIDTH

HY_ORDER = 2
POS_EMB_DIM = 33
FILTER_HIDDEN = 64
FILTER_SIN_W = 1.0
DECAY_FAST_PCT = 0.3
DECAY_SLOW_PCT = 1.5
DECAY_TARGET = 1e-2

N_EXPERTS = 64
TOP_K = 8
N_GROUPS = 8
TOPK_GROUPS = 4
D_EXPERT = 256
D_SHARED = 256
ROUTED_SCALE = 2.5

kernel_name = 'hybrid_diffattn_mlstm_hyena_moe_dit'

f32 = jnp.float32

def _rms(x, g):
    xf = x.astype(f32)
    y = xf * lax.rsqrt(jnp.mean(xf * xf, axis=-1, keepdims=True) + RMS_EPS)
    return (y * g.astype(f32)).astype(x.dtype)

def _rms_heads(o, n_heads, g):
    B, L, W = o.shape
    of = o.astype(f32).reshape(B, L, n_heads, W // n_heads)
    of = of * lax.rsqrt(jnp.mean(of * of, axis=-1, keepdims=True) + RMS_EPS)
    return (of.reshape(B, L, W) * g.astype(f32)).astype(o.dtype)

def _modulate(h, shift, scale):
    return h * (1 + scale[:, None, :]) + shift[:, None, :]

def _split(t, widths):
    idx, acc = [], 0
    for w in widths[:-1]:
        acc += w
        idx.append(acc)
    return jnp.split(t, idx, axis=-1)

def _dwconv_centred(x, w, b):
    K = w.shape[0]
    L = x.shape[1]
    xp = jnp.pad(x, ((0, 0), (K // 2, K // 2), (0, 0)))
    return sum(xp[:, j:j + L] * w[j] for j in range(K)) + b

def _axial_rope(L):
    rows = L // GRID_W
    row = jnp.repeat(jnp.arange(rows), GRID_W)
    col = jnp.tile(jnp.arange(GRID_W), rows)
    inv = ROPE_BASE ** (-jnp.arange(ROPE_AXIS_PAIRS, dtype=f32) / ROPE_AXIS_PAIRS)
    ang = jnp.stack([row, col], axis=-1).astype(f32)[..., None] * inv
    ang = jnp.broadcast_to(ang[:, :, None, :], (L, 2, 2, ROPE_AXIS_PAIRS)).reshape(L, A_DQK)
    return jnp.cos(ang), jnp.sin(ang)

def _rope_2d(x, cos, sin):
    xa = x.reshape(*x.shape[:-1], 2, 2, ROPE_AXIS_PAIRS)
    rot = jnp.concatenate([-xa[..., 1:, :], xa[..., :1, :]], axis=-2).reshape(x.shape)
    c = cos[None, :, None, None, :].astype(x.dtype)
    s = sin[None, :, None, None, :].astype(x.dtype)
    return x * c + rot * s

def _diff_attention(q, k, v, lam):
    B, S, H = q.shape[:3]
    nb = S // Q_BLOCK
    qb = jnp.moveaxis(q.reshape(B, nb, Q_BLOCK, H, 2, A_DQK), 1, 0)

    def one_block(qi):
        s = jnp.einsum('bqhcd,bkhcd->bhcqk', qi, k).astype(f32) * (A_DQK ** -0.5)
        p = jax.nn.softmax(s, axis=-1)
        a = (p[:, :, 0] - lam * p[:, :, 1]).astype(v.dtype)
        return jnp.einsum('bhqk,bkhd->bqhd', a, v)

    o = lax.map(one_block, qb)
    return jnp.moveaxis(o, 0, 1).reshape(B, S, H * A_DV)

def _to_heads(t, n_heads):
    B, L, W = t.shape
    return t.astype(f32).reshape(B, L, n_heads, W // n_heads).transpose(0, 2, 1, 3)

def _gate_logs(g):
    B, L, _ = g.shape
    g = g.astype(f32).reshape(B, L, 2, 2, B_HEADS).transpose(0, 2, 3, 4, 1)
    return g[:, :, 0], jax.nn.log_sigmoid(g[:, :, 1])

def _mlstm_absorb(state, k, v, li, lf):
    C, n, m = state
    b = jnp.cumsum(lf, axis=-1)
    bL = b[..., -1]
    g = bL[..., None] - b + li
    m_new = jnp.maximum(bL + m, jnp.max(g, axis=-1))
    w = jnp.exp(g - m_new[..., None])
    decay = jnp.exp(bL + m - m_new)
    C = decay[..., None, None] * C + jnp.einsum('bhsd,bhse->bhde', k * w[..., None], v)
    n = decay[..., None] * n + jnp.einsum('bhs,bhsd->bhd', w, k)
    return (C, n, m_new)

def _mlstm_chunkwise(q, k, v, li, lf, state):
    B, H, L, dk = q.shape
    nc = L // CHUNK

    def chunks(a):
        return jnp.moveaxis(a.reshape(B, H, nc, CHUNK, *a.shape[3:]), 2, 0)

    causal = jnp.tril(jnp.ones((CHUNK, CHUNK), dtype=bool))

    def step(carry, inp):
        C, n, m = carry
        qc, kc, vc, ic, fc = inp
        b = jnp.cumsum(fc, axis=-1)
        d = jnp.where(causal, b[..., :, None] - b[..., None, :] + ic[..., None, :], -jnp.inf)
        inter = b + m[..., None]
        m_t = jnp.maximum(inter, jnp.max(d, axis=-1))
        s = jnp.einsum('bhtd,bhsd->bhts', qc, kc) * jnp.exp(d - m_t[..., None])
        sc = jnp.exp(inter - m_t)
        num = sc[..., None] * jnp.einsum('bhtd,bhde->bhte', qc, C) + jnp.einsum('bhts,bhse->bhte', s, vc)
        den = sc * jnp.einsum('bhtd,bhd->bht', qc, n) + jnp.sum(s, axis=-1)
        h = num / jnp.maximum(jnp.abs(den), jnp.exp(-m_t))[..., None]
        return _mlstm_absorb((C, n, m), kc, vc, ic, fc), h

    _, h = lax.scan(step, state, (chunks(q), chunks(k), chunks(v), chunks(li), chunks(lf)))
    return jnp.moveaxis(h, 0, 2).reshape(B, H, L, v.shape[-1])

def _flip(a, rev):
    return jnp.flip(a, axis=2) if rev else a

def _mlstm_bidirectional(q, k, v, gts, ck, cv, cgts):
    B, S, _ = q.shape
    q = _to_heads(q, B_HEADS) * (B_DH ** -0.5)
    k, v = _to_heads(k, B_HEADS), _to_heads(v, B_HEADS)
    ck, cv = _to_heads(ck, B_HEADS), _to_heads(cv, B_HEADS)
    li, lf = _gate_logs(gts)
    cli, clf = _gate_logs(cgts)
    zero = (jnp.zeros((B, B_HEADS, B_DH, B_DH), f32), jnp.zeros((B, B_HEADS, B_DH), f32),
            jnp.zeros((B, B_HEADS), f32))
    out = 0.0
    for d in range(2):
        rev = d == 1
        st = _mlstm_absorb(zero, _flip(ck, rev), _flip(cv, rev), _flip(cli[:, d], rev), _flip(clf[:, d], rev))
        hd = _mlstm_chunkwise(_flip(q, rev), _flip(k, rev), _flip(v, rev),
                              _flip(li[:, d], rev), _flip(lf[:, d], rev), st)
        out = out + _flip(hd, rev)
    return out.transpose(0, 2, 1, 3).reshape(B, S, B_WIDTH)

def _ab_mixer(h, hc, w_in, conv_w, conv_b, gate_b, lam_vecs, g_a, g_b, w_out, lam_init):
    B, S, _ = h.shape
    Lc = hc.shape[1]
    a_q, b_q, b_o, a_k, a_v, b_k, b_v, b_g = _split(
        h @ w_in, (A_QW, B_WIDTH, B_WIDTH, A_QW, A_VW, B_WIDTH, B_WIDTH, GATE_W))
    ca_k, ca_v, cb_k, cb_v, cb_g = _split(hc @ w_in[:, Q_SIDE:], (A_QW, A_VW, B_WIDTH, B_WIDTH, GATE_W))

    cos, sin = _axial_rope(S)
    q = _rope_2d(a_q.reshape(B, S, A_HEADS, 2, A_DQK), cos, sin)
    k_lat = _rope_2d(a_k.reshape(B, S, A_HEADS, 2, A_DQK), cos, sin)
    keys = jnp.concatenate([ca_k.reshape(B, Lc, A_HEADS, 2, A_DQK), k_lat], axis=1)
    vals = jnp.concatenate([ca_v.reshape(B, Lc, A_HEADS, A_DV), a_v.reshape(B, S, A_HEADS, A_DV)], axis=1)
    lv = lam_vecs.astype(f32)
    lam = jnp.exp(jnp.sum(lv[0] * lv[1])) - jnp.exp(jnp.sum(lv[2] * lv[3])) + lam_init
    out_a = _rms_heads(_diff_attention(q, keys, vals, lam), A_HEADS, g_a) * (1.0 - lam_init)

    qk = jax.nn.silu(_dwconv_centred(jnp.concatenate([b_q, b_k], axis=-1), conv_w, conv_b))
    mq, mk = jnp.split(qk, 2, axis=-1)
    cmk = jax.nn.silu(_dwconv_centred(cb_k, conv_w[:, B_WIDTH:], conv_b[B_WIDTH:]))
    hb = _mlstm_bidirectional(mq, mk, b_v, b_g + gate_b, cmk, cb_v, cb_g + gate_b)
    out_b = _rms_heads(hb.astype(h.dtype), B_HEADS, g_b) * jax.nn.sigmoid(b_o)

    return jnp.concatenate([out_a, out_b], axis=-1) @ w_out

def _hyena_filters(L, fw1, fb1, fw2, fb2, fw3):
    j = jnp.arange(L, dtype=f32)
    bands = (POS_EMB_DIM - 1) // 2
    freqs = jnp.linspace(1e-4, bands - 1, bands, dtype=f32)
    ang = (2.0 * math.pi / L) * j[:, None] * freqs[None, :]
    z = jnp.concatenate([(j / (L - 1))[:, None], jnp.cos(ang), -jnp.sin(ang)], axis=-1)
    hid = jnp.sin(FILTER_SIN_W * (z @ fw1.astype(f32) + fb1.astype(f32)))
    hid = jnp.sin(FILTER_SIN_W * (hid @ fw2.astype(f32) + fb2.astype(f32)))
    filt = (hid @ fw3.astype(f32)).reshape(L, HY_ORDER, D_MODEL)
    dist = jnp.abs(j - L // 2) / (L // 2)
    max_decay = math.log(DECAY_TARGET) / DECAY_FAST_PCT
    min_decay = math.log(DECAY_TARGET) / DECAY_SLOW_PCT
    deltas = jnp.abs(jnp.linspace(min_decay, max_decay, D_MODEL, dtype=f32))
    window = jnp.exp(-dist[:, None] * deltas[None, :])
    return filt * window[:, None, :]

def _fft_conv_centred(u, filt):
    L = u.shape[1]
    n = 2 * L
    U = jnp.fft.rfft(u.astype(f32), n=n, axis=1)
    K = jnp.fft.rfft(filt.astype(f32), n=n, axis=0)
    y = jnp.fft.irfft(U * K[None], n=n, axis=1)[:, L // 2:L // 2 + L]
    return y.astype(u.dtype)

def _hyena_mixer(h, w_in, conv_w, conv_b, fw1, fb1, fw2, fb2, fw3, fbias, w_out):
    L = h.shape[1]
    u = _dwconv_centred(h @ w_in, conv_w, conv_b)
    v, x1, x2 = jnp.split(u, 3, axis=-1)
    filt = _hyena_filters(L, fw1, fb1, fw2, fb2, fw3)
    z = x1 * (_fft_conv_centred(v, filt[:, 0]) + v * fbias[0])
    y = x2 * (_fft_conv_centred(z, filt[:, 1]) + z * fbias[1])
    return y @ w_out

def _swiglu(t, w_gu, w_dn):
    gate, up = jnp.split(t @ w_gu, 2, axis=-1)
    return (jax.nn.silu(gate) * up) @ w_dn

def _moe(h, router_w, router_b, exp_gu, exp_down, sh_gu, sh_down):
    B, L, D = h.shape
    t = h.reshape(B * L, D)
    T = t.shape[0]
    scores = jax.nn.sigmoid((t @ router_w).astype(f32))
    biased = scores + router_b.astype(f32)
    grp = lax.top_k(biased.reshape(T, N_GROUPS, N_EXPERTS // N_GROUPS), 2)[0].sum(-1)
    _, gidx = lax.top_k(grp, TOPK_GROUPS)
    gmask = jax.nn.one_hot(gidx, N_GROUPS, dtype=f32).sum(-2) > 0
    emask = jnp.repeat(gmask, N_EXPERTS // N_GROUPS, axis=-1)
    _, eidx = lax.top_k(jnp.where(emask, biased, -jnp.inf), TOP_K)
    sel = jnp.take_along_axis(scores, eidx, axis=-1)
    wts = ROUTED_SCALE * sel / jnp.sum(sel, axis=-1, keepdims=True)
    gates = jnp.zeros((T, N_EXPERTS), f32).at[jnp.arange(T)[:, None], eidx].set(wts)

    def expert_step(acc, e):
        gu_e, dn_e, g_e = e
        return acc + g_e[:, None] * _swiglu(t, gu_e, dn_e), None

    routed, _ = lax.scan(expert_step, jnp.zeros_like(t), (exp_gu, exp_down, gates.T.astype(t.dtype)))
    return (_swiglu(t, sh_gu, sh_down) + routed).reshape(B, L, D)

def setup_inputs(seed: int = 0) -> dict:
    key = jax.random.key(seed)
    ks = iter(jax.random.split(key, 40))

    def nrm(shape, scale):
        return jax.random.normal(next(ks), shape, f32) * scale

    D = D_MODEL
    i_b = nrm((N_EVEN, 2, 1, B_HEADS), 0.1)
    f_b = jnp.linspace(3.0, 6.0, B_HEADS, dtype=f32)[None, None, None, :] + nrm((N_EVEN, 2, 1, B_HEADS), 0.1)
    return {
        'x': nrm((BATCH, SEQ, D), 1.0),
        'c': nrm((BATCH, D), 1.0),
        'ctx': nrm((BATCH, CTX_LEN, D), 1.0),
        'c_ctx': nrm((D,), 1.0),
        'w_mod': nrm((DEPTH, D, N_MOD * D), 0.5 * D ** -0.5),
        'b_mod': nrm((DEPTH, N_MOD * D), 0.02),
        'norm_g': 1.0 + nrm((DEPTH, 4, D), 0.05),
        'w_in_ab': nrm((N_EVEN, D, P_AB), D ** -0.5),
        'conv_ab_w': nrm((N_EVEN, SHORT_CONV, 2 * B_WIDTH), SHORT_CONV ** -0.5),
        'conv_ab_b': nrm((N_EVEN, 2 * B_WIDTH), 0.02),
        'gate_b_ab': jnp.concatenate([i_b, f_b], axis=2).reshape(N_EVEN, GATE_W),
        'diff_lambda': nrm((N_EVEN, 4, A_DQK), 0.1),
        'head_g_a': 1.0 + nrm((N_EVEN, A_VW), 0.05),
        'head_g_b': 1.0 + nrm((N_EVEN, B_WIDTH), 0.05),
        'w_out_ab': nrm((N_EVEN, MIX_W, D), MIX_W ** -0.5),
        'w_in_hy': nrm((N_ODD, D, 3 * D), D ** -0.5),
        'conv_hy_w': nrm((N_ODD, SHORT_CONV, 3 * D), SHORT_CONV ** -0.5),
        'conv_hy_b': nrm((N_ODD, 3 * D), 0.02),
        'filt_w1': nrm((N_ODD, POS_EMB_DIM, FILTER_HIDDEN), POS_EMB_DIM ** -0.5),
        'filt_b1': nrm((N_ODD, FILTER_HIDDEN), 0.1),
        'filt_w2': nrm((N_ODD, FILTER_HIDDEN, FILTER_HIDDEN), FILTER_HIDDEN ** -0.5),
        'filt_b2': nrm((N_ODD, FILTER_HIDDEN), 0.1),
        'filt_w3': nrm((N_ODD, FILTER_HIDDEN, HY_ORDER * D), 0.1 * FILTER_HIDDEN ** -0.5),
        'filt_bias': nrm((N_ODD, HY_ORDER, D), 0.1),
        'w_out_hy': nrm((N_ODD, D, D), D ** -0.5),
        'router_w': nrm((DEPTH, D, N_EXPERTS), D ** -0.5),
        'router_b': nrm((DEPTH, N_EXPERTS), 0.01),
        'exp_gu': nrm((DEPTH, N_EXPERTS, D, 2 * D_EXPERT), D ** -0.5),
        'exp_down': nrm((DEPTH, N_EXPERTS, D_EXPERT, D), D_EXPERT ** -0.5),
        'sh_gu': nrm((DEPTH, D, 2 * D_SHARED), D ** -0.5),
        'sh_down': nrm((DEPTH, D_SHARED, D), D_SHARED ** -0.5),
    }

def reference(x, c, ctx, c_ctx, w_mod, b_mod, norm_g, w_in_ab, conv_ab_w, conv_ab_b, gate_b_ab,
              diff_lambda, head_g_a, head_g_b, w_out_ab, w_in_hy, conv_hy_w, conv_hy_b,
              filt_w1, filt_b1, filt_w2, filt_b2, filt_w3, filt_bias, w_out_hy,
              router_w, router_b, exp_gu, exp_down, sh_gu, sh_down):
    silu_c = jax.nn.silu(c)
    silu_cc = jax.nn.silu(c_ctx)
    for l in range(DEPTH):
        mod = silu_c @ w_mod[l] + b_mod[l]
        sh_m, sc_m, g_m, sh_f, sc_f, g_f = jnp.split(mod, N_MOD, axis=-1)
        h = _modulate(_rms(x, norm_g[l, 0]), sh_m, sc_m)
        if l % 2 == 0:
            e = l // 2
            lam_init = 0.8 - 0.6 * math.exp(-0.3 * l)
            mod_c = silu_cc @ w_mod[l, :, :2 * D_MODEL] + b_mod[l, :2 * D_MODEL]
            shift_c, scale_c = jnp.split(mod_c, 2)
            hc = _rms(ctx, norm_g[l, 0]) * (1 + scale_c) + shift_c
            mix = _ab_mixer(h, hc, w_in_ab[e], conv_ab_w[e], conv_ab_b[e], gate_b_ab[e], diff_lambda[e],
                            head_g_a[e], head_g_b[e], w_out_ab[e], lam_init)
        else:
            o = l // 2
            mix = _hyena_mixer(h, w_in_hy[o], conv_hy_w[o], conv_hy_b[o], filt_w1[o], filt_b1[o],
                               filt_w2[o], filt_b2[o], filt_w3[o], filt_bias[o], w_out_hy[o])
        x = x + g_m[:, None, :] * _rms(mix, norm_g[l, 1])
        h = _modulate(_rms(x, norm_g[l, 2]), sh_f, sc_f)
        x = x + g_f[:, None, :] * _rms(_moe(h, router_w[l], router_b[l], exp_gu[l], exp_down[l],
                                            sh_gu[l], sh_down[l]), norm_g[l, 3])
    return x


_drawn_inputs = setup_inputs


def setup_inputs(seed=0):
    import zlib

    import numpy as np

    out = dict(_drawn_inputs(seed))
    spreads = {}
    factors = {'conv_ab_b': 4.459}
    for name, (base, spread) in spreads.items():
        noise = np.random.default_rng([zlib.crc32(name.encode()), seed]).standard_normal(out[name].shape)
        drawn = base * np.exp(spread * noise) if base else spread * noise
        out[name] = __import__('jax').numpy.asarray(drawn.astype(out[name].dtype))
    for name, factor in factors.items():
        out[name] = (out[name] * factor).astype(out[name].dtype)
    return out
```

```python
import concourse.bass as bass
from concourse import mybir
from contextlib import ExitStack
import math
import numpy as np

F32 = mybir.dt.float32
BF16 = mybir.dt.bfloat16
I32 = mybir.dt.int32
ALU = mybir.AluOpType
ACT = mybir.ActivationFunctionType
AX_X = mybir.AxisListType.X

P = 128
D = 1024
KT = D // P
T = 256
TT = T // P
NB = 512
HALVES = D // NB
HEADS = 4
DQK = 64
DV = 128
POS_DIM, HIDDEN = 33, 64
E = 64
NG = 8
F = 256
C = 64
OVER = 32
PAIRS = E // 2
FREQ = 256
EPS = 1e-6
LAM_INIT = 0.2
BIG = 1e30

C_IDENT, C_ROT, C_TRI, C_ONES = 0, 128, 256, 384
C_COS, C_SIN = 640, 896
C_SLOT, C_K, C_E, C_ROW8, C_END = 1152, 1216, 1248, 1249, 1257
Q_C, Q_CC = 0, 8
Q_CAW, Q_CAB = 16, 40
Q_CHW, Q_CHB = 48, 120
Q_FB, Q_GB, Q_LV = 144, 160, 162
Q_W1, Q_W2, Q_B = 166, 230, 294
Q_END = 296


def shape_constants():
    small = np.zeros((P, C_END), np.float32)
    small[:, C_IDENT:C_IDENT + P] = np.eye(P)
    for m in range(P):
        low = m % 32 < 16
        small[m + 16 if low else m - 16, C_ROT + m] = -1.0 if low else 1.0
    small[:, C_TRI:C_TRI + P] = np.triu(np.ones((P, P)))
    small[:, C_ONES:C_ONES + T] = 1.0
    pairs = DQK // 4
    inv = (np.float32(10000.0) ** (-np.arange(pairs, dtype=np.float32) / pairs)).astype(np.float32)
    tok = np.arange(T)
    place = np.stack([tok // 64, tok % 64], -1).astype(np.float32)
    ang = place[..., None] * inv
    ang = np.broadcast_to(ang[:, :, None, :], (T, 2, 2, pairs)).reshape(T, DQK)
    small[:, C_COS:C_COS + T] = np.tile(np.cos(ang).T, (2, 1))
    small[:, C_SIN:C_SIN + T] = np.tile(np.sin(ang).T, (2, 1))
    small[:, C_SLOT:C_SLOT + C] = np.arange(1, C + 1)
    small[:, C_K:C_K + OVER] = np.arange(OVER)
    small[:, C_E] = np.arange(P)
    rows = [32 * d + h for d in range(2) for h in range(HEADS)]
    for r, row in enumerate(rows):
        small[row, C_ROW8 + r] = 1.0
    pick = np.zeros((P, 8, P), np.float32)
    for r, row in enumerate(rows):
        pick[row, r, :] = 1.0
    mask = np.zeros((P, 2, TT, 2 * T), np.float32)
    t = np.arange(T).reshape(TT, P).T[:, :, None]
    s = np.arange(T)[None, None, :]
    mask[:, 0, :, T:] = np.where(s <= t, 0.0, -BIG)
    mask[:, 1, :, T:] = np.where(s >= t, 0.0, -BIG)
    w = 2 * np.pi * (np.arange(FREQ) + 0.5) / (2 * FREQ)
    fwd = np.concatenate([np.cos(np.outer(np.arange(T), w)), -np.sin(np.outer(np.arange(T), w))], 1)
    fwd = fwd.reshape(TT, P, 2 * FREQ).transpose(1, 0, 2)
    late = np.arange(T) + T // 2
    inv_ = np.concatenate([np.cos(np.outer(w, late)), -np.sin(np.outer(w, late))], 0) / FREQ
    inv_ = inv_.reshape(4, P, T).transpose(1, 0, 2)
    dft = np.concatenate([fwd.reshape(P, -1), inv_.reshape(P, -1)], 1).astype(np.float32)
    f = np.float32
    j = np.arange(T, dtype=f)
    bands = (POS_DIM - 1) // 2
    freqs = np.linspace(1e-4, bands - 1, bands, dtype=f)
    a = (f(2.0 * math.pi / T) * j[:, None] * freqs[None, :]).astype(f)
    z = np.concatenate([(j / (T - 1))[:, None], np.cos(a), -np.sin(a)], -1)
    zt = np.zeros((P, T), f)
    zt[:POS_DIM] = z.T
    dist = np.abs(j - T // 2) / (T // 2)
    deltas = np.abs(np.linspace(math.log(1e-2) / 1.5, math.log(1e-2) / 0.3, D, dtype=f))
    window = np.exp(-dist[:, None] * deltas[None, :]).astype(f)
    window = window.reshape(TT, P, D).transpose(1, 0, 2)
    return {"k_small": small, "k_pick": pick.reshape(P, -1), "k_mask": mask.reshape(P, -1), "k_dft": dft,
            "k_pos": zt, "k_window": np.ascontiguousarray(window).reshape(P, -1)}


def build(nc, a, out):
    with ExitStack() as ctx:
        def sb(name, shape, dt=F32):
            return ctx.enter_context(nc.sbuf_tensor(name, shape, dt))

        def sem(name):
            return ctx.enter_context(nc.semaphore(name))

        bank = ctx.enter_context(nc.psum_tensor("bank", [P, 8, NB], F32))
        gu = sb("gu", [P, 4, KT, NB])
        dn = sb("dn", [P, 4, 2, D])
        zone = sb("zone", [P, 10240])
        x = sb("x", [P, TT, D])
        hh = sb("hh", [P, TT, D])
        hc = sb("hc", [P, KT, T])
        hl = sb("hl", [P, KT, T])
        mod = sb("mod", [P, 6, D])
        bn = sb("bn", [P, 2, NB])
        cbc = sb("cbc", [P, KT, P])
        small = sb("small", [P, C_END])
        par = sb("par", [P, Q_END])
        st = sb("st", [P, 128])

        def const(c, n=P):
            return small[:, c:c + n]

        ident, ones = const(C_IDENT), const(C_ONES)
        cos, sin = const(C_COS, T), const(C_SIN, T)
        off = [0]

        def zv(n, shape, at=None, dt=F32):
            o = off[0] if at is None else at
            off[0] = o + n
            assert off[0] <= 10240
            v = zone[:, o:o + n]
            if dt != F32:
                v = v.bitcast(dt)
            if len(shape) == 1:
                return v
            names = "abcd"[:len(shape)]
            return v.rearrange(f"p ({' '.join(names)}) -> p {' '.join(names)}", **dict(zip(names, shape)))

        def dv(i, shape):
            names = "abcd"[:len(shape)]
            return dn[:, i].rearrange("p f n -> p (f n)").rearrange(
                f"p ({' '.join(names)}) -> p {' '.join(names)}", **dict(zip(names, shape)))

        qz = zv(2048, (2, HEADS, T), at=0)
        cx = zv(2048, (TT, D), at=0)
        qraw = zv(1024, (HEADS, T), at=2048)
        aT = zv(1024, (2, NB), at=2048)
        sgq = zv(1024, (HEADS, T), at=3072)
        amat = zv(1024, (2, NB), at=3072)
        bq = zv(1024, (HEADS, T), at=4096)
        sgk = zv(2048, (HEADS, 2 * T), at=5120)
        modc = zv(2048, (2, D), at=5120)
        cat = zv(2048, (TT, D), at=5120)
        sigbo = zv(1024, (TT, NB), at=7168)
        ccbc = zv(1024, (KT, P), at=7168)
        ex = zv(2048, (2, 2, NB), at=8192)
        wgz = zv(1024, (KT, 2, 64), at=8192)
        wgr = zv(128, (KT, 16), at=9216)
        rope = zv(512, (2, T), at=9344)
        kk = dv(0, (HEADS, 2 * T))
        av = dv(1, (4, NB))
        bv = dv(2, (4, NB))
        bk = dv(3, (HEADS, 2 * T))
        mask = hh[:, :, :].rearrange("p a (b n) -> p a b n", b=TT)
        pick = mod[:, 0, :].rearrange("p (r m) -> p r m", r=8)
        hgain = mod[:, 1, :].rearrange("p (g n) -> p g n", g=2)
        og = hc[:, :, :].rearrange("p k t -> p (k t)").rearrange("p (g n) -> p g n", g=4)

        ig, fg = ([zone[0:64, 8192 + 512 * j:8704 + 512 * j] for j in range(2)])
        lf, pre = mod[0:64, 1, 0:NB], mod[0:64, 1, NB:D]
        bnf = bn[:, :, :].rearrange("p a n -> p (a n)")
        decay_c, decay_b = bnf[:, 0:2 * T], bnf[:, 2 * T:3 * T]

        ut = zv(6144, (24, T), at=0)
        fw3 = zv(2048, (2 * D,), at=0)
        raw3 = hl[:, :, :]
        ys = zv(4096, (4, D), at=6144)
        filt = zv(4096, (TT, 2 * D), at=6144)
        kf = dn[:, :, :, :].rearrange("p r f n -> p r (f n)")
        dfc = hc[:, :, :].rearrange("p k t -> p (k t)")
        dfwd = dfc[:, 0:1024].rearrange("p (t f) -> p t f", t=TT)
        dinv = dfc[:, 1024:2048].rearrange("p (f t) -> p f t", f=4)
        window = hh[:, :, :]
        ztok = hh[:, :, :]

        th = zv(3072, (3, TT, D), at=0, dt=BF16)
        tg = zv(1024, (KT, P))
        ye = zv(1024, (2, NB))
        sg = zv(256, (F,))
        he = zv(256, (F,))
        hT = zv(256, (2, P))
        pm = zv(256, (T,))
        ptg = zv(256, (TT, P))
        ptb = zv(128, (TT, P), dt=BF16)
        pgc = zv(8, (2, 4))
        rw = zv(512, (KT, E))
        rb = zv(64, (E,))
        sc = zv(128, (TT, E))
        bi = zv(128, (TT, E))
        m8 = zv(128, (TT, NG, 8))
        g12 = zv(24, (TT, 12))
        g12r = zv(24, (TT, 12))
        top = zv(16, (TT, 8))
        gm = zv(16, (TT, NG))
        mk = zv(128, (TT, E))
        pg = zv(4 * (E + 4), (E + 4, 4))
        pgo = zv(4 * (OVER + 4), (OVER + 4, 4))
        over_at = off[0]
        nx = zv(4, (4,))
        sel = zv(2 * OVER, (2, OVER))
        pgT = zv(512, (4, P))
        over_tiles = zone[:, over_at:off[0]]
        eid = zv(40, (40,), dt=I32)

        s_const, s_tok, s_wg, s_ab = sem("constants_in"), sem("tokens_in"), sem("gate_w_in"), sem("ab_tables_in")
        chunk_in = [[sem(f"chunk_in{l}{s}") for s in range(4)] for l in range(2)]
        s_bn, s_silu, s_cbc = sem("mod_rows_in"), sem("silu_out"), sem("silu_spread")
        mod_ps, mod_out = sem("mod_ps"), sem("mod_out")
        nrm_ms, nrm_sd, nrm_h = sem("norm_square"), sem("norm_root"), sem("norm_out")
        hT_ps, hT_out = sem("features_ps"), sem("features_out")
        gate_w, gate_ps, gate_x, gate_l = sem("gate_w_rows"), sem("gates_ps"), sem("gates_abs"), sem("gates_log")
        gate_e = sem("gates_exp")
        crow = sem("decay_rows")
        bcol_ps, bcol_out = sem("decay_cols_ps"), sem("decay_cols_out")
        proj_ps, proj_out = sem("proj_ps"), sem("proj_out")
        rot_ps, rot_out, s_zero = sem("rot_ps"), sem("rot_out"), sem("query_zero")
        cv_y, cv_s, cv_out = sem("conv_sum"), sem("conv_sigmoid"), sem("conv_out")
        lam_p, lam_ps, lam_e = sem("lambda_products"), sem("lambda_ps"), sem("lambda_exp")
        score_ps, m_ready, e_ready, a_ready = sem("score_ps"), sem("max_out"), sem("exp_out"), sem("weights_out")
        at_ps, at_out, pv_ps, o_out = sem("wT_ps"), sem("wT_out"), sem("value_ps"), sem("heads_out")
        hn_ms, hn_sd, cat_out = sem("head_square"), sem("head_root"), sem("cat_out")
        cT_ps, cT_out = sem("catT_ps"), sem("catT_out")
        mix_ps, mix_sq, mix_ms, mix_sd, x_out = (
            sem("mix_ps"), sem("mix_square"), sem("mix_mean"), sem("mix_root"), sem("x_out"))
        s_hy = sem("hy_tables_in")
        f_ps, f_arg, f_sin = sem("filt_ps"), sem("filt_arg"), sem("filt_sin")
        ff_ps, ff_out, kf_ps, kf_out = sem("taps_ps"), sem("taps_out"), sem("spectra_ps"), sem("spectra_out")
        up_ps, up_out = sem("hy_proj_ps"), sem("hy_conv_out")
        vt_ps, vt_out, sp_ps, y_out = sem("hy_T_ps"), sem("hy_T_out"), sem("hy_spec_ps"), sem("hy_prod_out")
        iv_ps, z_out = sem("hy_inv_ps"), sem("hy_gated_out")
        r_in, r_ps, r_sc = sem("router_in"), sem("router_ps"), sem("router_scores")
        r_mk, r_cu, r_pg = sem("router_mask"), sem("router_count_ps"), sem("router_slots")
        r_nx, r_of, r_sel = sem("over_counts"), sem("over_offset_ps"), sem("over_select")
        r_tp, r_to, r_ov, r_id = sem("slotsT_ps"), sem("slotsT_out"), sem("over_ps"), sem("over_ready")
        split_out = sem("split_out")
        sh_ps, sh_sig, sh_h = sem("shared_ps"), sem("shared_sigmoid"), sem("shared_h")
        sh_tp, sh_to, sh_dn = sem("sharedT_ps"), sem("sharedT_out"), sem("shared_down_ps")
        dn_in = sem("shared_down_in")
        over_free = sem("further_done")
        s_out = sem("out_written")
        dve_step = sem("dve_step")
        pool_step = sem("pool_step")

        class Pairs:

            def __init__(self, name, slot_pairs):
                self.gu_in = [sem(f"{name}_gu_in{b}") for b in range(slot_pairs)]
                self.dn_in = [sem(f"{name}_dn_in{b}") for b in range(slot_pairs)]
                self.built, self.step = sem(f"{name}_slots_built"), sem(f"{name}_build_step")
                self.g_ps, self.g_out = sem(f"{name}_gather_ps"), sem(f"{name}_gather_out")
                self.gu_ps, self.sig = sem(f"{name}_gu_ps"), sem(f"{name}_sigmoid")
                self.h, self.hs = sem(f"{name}_h"), sem(f"{name}_h_step")
                self.hT_ps, self.hT_out = sem(f"{name}_hT_ps"), sem(f"{name}_hT_out")
                self.y_ps, self.y_out = sem(f"{name}_y_ps"), sem(f"{name}_y_out")
                self.pT_ps, self.pT_out = sem(f"{name}_pT_ps"), sem(f"{name}_pT_out")

        first = Pairs("first", 2)
        further = [Pairs(f"further{l}", 1) for l in range(2)]

        block = ctx.enter_context(nc.Block())
        N_AB = [4, 4, 2, 4, 4, 4, 4]
        CHUNKS = ([("mod", n) for n in range(12)] + [("in", n) for n in range(7)] + [("out", 0), ("out", 1), ("sh", 0)],
                  [("mod", n) for n in range(12)] + [("in", n) for n in range(6)] + [("out", 0), ("out", 1), ("sh", 0)])
        SHIFT = [0, 2]
        w_mod = [a["w_mod"][l].rearrange("(k p) n -> p k n", p=P) for l in range(2)]
        w_in = [a["w_in_ab"][0].rearrange("(k p) n -> p k n", p=P), a["w_in_hy"][0].rearrange("(k p) n -> p k n", p=P)]
        w_out = [a["w_out_ab"][0].rearrange("(k p) n -> p k n", p=P), a["w_out_hy"][0].rearrange("(k p) n -> p k n", p=P)]

        def slot_of(l, n):
            return (n + SHIFT[l]) % 4

        def chunk_ready(eng, l, n):
            eng.wait_ge(chunk_in[l][slot_of(l, n)], 16 * (n // 4 + 1))

        def chunk_index(l, kind, n):
            return CHUNKS[l].index((kind, n))

        def unit_read(u):
            if u < 4:
                return proj_out, u + 1
            if u < 8:
                return cv_y, u - 3
            if u < 18:
                return proj_out, u - 3
            if u < 22:
                return cv_y, u - 13
            return proj_out, u - 7

        def chunk_used(l, n):
            kind, c = CHUNKS[l][n]
            if kind == "mod":
                return mod_ps, 12 * l + c + 1
            if kind == "in":
                return (proj_ps, sum(N_AB[:c + 1])) if l == 0 else (up_ps, 4 * (c + 1))
            if kind == "out":
                return mix_ps, 4 * l + 2 * (c + 1)
            return sh_ps, 2 * (l + 1)

        @block.sync
        def _(sp):
            sp.dma_start(small[:, :], a["k_small"]).then_inc(s_const, 16)
            sp.dma_start(par[:, :], a["params"]).then_inc(s_const, 16)
            sp.dma_start(cx[:, :, :], a["ctx"][0].rearrange("(t p) d -> p t d", p=P)).then_inc(s_tok, 16)
            sp.dma_start(x[:, :, :], a["x"][0].rearrange("(t p) d -> p t d", p=P)).then_inc(s_tok, 16)

            def chunks(l):
                for n, (kind, c) in enumerate(CHUNKS[l]):
                    if n >= 4:
                        sp.wait_ge(*chunk_used(l, n - 4))
                    elif l == 1 and n < 2:
                        sp.wait_ge(first.gu_ps, PAIRS)
                    elif l == 1 and n == 2:
                        sp.wait_ge(over_free, 1)
                    cols = slice(c * NB, (c + 1) * NB)
                    src = {"mod": w_mod[l], "in": w_in[l], "out": w_out[l]}
                    src = a["sh_gu"][l].rearrange("(k p) n -> p k n", p=P) if kind == "sh" else src[kind][:, :, cols]
                    s = slot_of(l, n)
                    sp.dma_start(gu[:, s], src).then_inc(chunk_in[l][s], 16)
                if l == 0:
                    sp.wait_ge(pv_ps, 16)
                else:
                    sp.wait_ge(y_out, 4)
                sp.dma_start(dn[:, 3], a["sh_down"][l].rearrange("(f p) n -> p f n", p=P)).then_inc(dn_in, 16)

            def expert(l, e, j, ph):
                gu_src, dn_src = a["exp_gu"][l], a["exp_down"][l]
                sp.dma_start(gu[:, j], gu_src[bass.ds(e, 1)].rearrange("a (k p) n -> p (a k) n", p=P)).then_inc(
                    ph.gu_in[j // 2], 16)

            def expert_down(l, e, j, ph):
                sp.dma_start(dn[:, j], a["exp_down"][l][bass.ds(e, 1)].rearrange("a (f p) n -> p (a f) n", p=P)).then_inc(
                    ph.dn_in[j // 2], 16)

            for l in range(2):
                chunks(l)
                last = len(CHUNKS[l])
                for b in range(2):
                    for j in range(2):
                        s = 2 * b + j
                        n = max(m for m in range(last) if slot_of(l, m) == s)
                        sp.wait_ge(*chunk_used(l, n))
                        expert(l, s, s, first)
                        if b == 1:
                            sp.wait_ge(sh_dn, l + 1)
                        expert_down(l, s, s, first)
                with sp.Fori(1, PAIRS // 2) as i:
                    for b in range(2):
                        sp.wait_ge(first.gu_ps, 2 * i + (b - 1 + PAIRS * l))
                        expert(l, 4 * i + 2 * b, 2 * b, first)
                        expert(l, 4 * i + (2 * b + 1), 2 * b + 1, first)
                        sp.wait_ge(first.y_ps, 4 * i + 2 * (b - 1 + PAIRS * l))
                        expert_down(l, 4 * i + 2 * b, 2 * b, first)
                        expert_down(l, 4 * i + (2 * b + 1), 2 * b + 1, first)
                ph = further[l]
                sp.wait_ge(r_id, l + 1)
                sp.wait_ge(first.gu_ps, PAIRS * (l + 1) - 1)
                sp.wait_ge(first.y_ps, 2 * (PAIRS * (l + 1) - 1))
                n = sp.value_load(eid[0:1, 36:37], min_val=1, max_val=OVER // 2)
                with sp.Fori(0, n) as i:
                    sp.wait_ge(ph.gu_ps, i + 1)
                    es = [sp.value_load(eid[0:1, bass.ds(2 * i + j, 1)], min_val=0, max_val=E - 1) for j in range(2)]
                    for j in range(2):
                        expert(l, es[j], j, ph)
                    sp.wait_ge(ph.y_ps, 2 * i + 2)
                    for j in range(2):
                        expert_down(l, es[j], j, ph)
            sp.wait_ge(x_out, 8)
            sp.dma_start(out[0].rearrange("(t p) d -> p t d", p=P), x[:, :, :]).then_inc(s_out, 16)
            sp.wait_ge(s_out, 16)

        @block.gpsimd
        def _(pool):
            steps = [0]

            def step(ins):
                steps[0] += 1
                ins.then_inc(pool_step, 1)
                pool.wait_ge(pool_step, steps[0])

            def mod_rows(l):
                for n in range(12):
                    if n or l:
                        pool.wait_ge(mod_out, 12 * l + n)
                    cols = slice(n * NB, (n + 1) * NB)
                    src = a["b_mod"][l, cols].rearrange("(o n) -> o n", o=1)
                    pool.dma_start(bn[:, 0, :], src.broadcast_to([P, NB])).then_inc(s_bn, 16)
                    g = {1: 0, 2: 1, 4: 2, 5: 3}.get(n // 2)
                    if g is not None:
                        cols = slice((n % 2) * NB, (n % 2 + 1) * NB)
                        src = a["norm_g"][l, g, cols].rearrange("(o n) -> o n", o=1)
                        pool.dma_start(bn[:, 1, :], src.broadcast_to([P, NB])).then_inc(s_bn, 16)

            def router_loads(l):
                pool.wait_ge(x_out, 4 * l + 2)
                pool.dma_start(rw, a["router_w"][l].rearrange("(k p) e -> p k e", p=P)).then_inc(r_in, 16)
                pool.dma_start(rb, a["router_b"][l:l + 1].broadcast_to([P, E])).then_inc(r_in, 16)

            def moe(l):
                for t in range(TT):
                    pool.wait_ge(nrm_h, 2 * (2 if l == 0 else 4) + t + 1)
                    pool.wait_ge(hT_ps, 2 * (2 * (2 if l == 0 else 4) + t + 1))
                    for q in range(3):
                        if q < 2:
                            step(nc.gpsimd.tensor_copy(th[:, q, t, :], hh[:, t, :]))
                            step(nc.gpsimd.tensor_tensor(hh[:, t, :], hh[:, t, :], th[:, q, t, :], ALU.subtract))
                        else:
                            nc.gpsimd.tensor_copy(th[:, q, t, :], hh[:, t, :]).then_inc(split_out, 1)

            mod_rows(0)
            pool.wait_ge(nrm_h, 4)
            pool.dma_start(mod[:, 0, :], a["k_pick"]).then_inc(s_ab, 16)
            nc.gpsimd.memset(qz[:, :, :, :].rearrange("p a b c -> p (a b c)"), 0.0).then_inc(s_zero, 1)
            pool.wait_ge(hT_ps, 8)
            pool.dma_start(mask, a["k_mask"].rearrange("p (a b n) -> p a b n", a=2, b=TT)).then_inc(s_ab, 16)
            pool.wait_ge(crow, 1)
            for g, name in enumerate(("head_g_a", "head_g_b")):
                pool.dma_start(hgain[:, g, :], a[name][0:1].broadcast_to([P, NB])).then_inc(s_ab, 16)
            router_loads(0)
            moe(0)
            pool.wait_ge(x_out, 4)
            pool.dma_start(window, a["k_window"].rearrange("p (t n) -> p t n", t=TT)).then_inc(s_hy, 16)
            pool.dma_start(fw3, a["filt_w3"]).then_inc(s_hy, 16)
            pool.dma_start(raw3[:, 0, :], a["k_pos"]).then_inc(s_hy, 16)
            pool.dma_start(dfc, a["k_dft"]).then_inc(s_hy, 16)
            mod_rows(1)
            router_loads(1)
            moe(1)

        @block.tensor
        def _(pe):
            def mm(o, lhsT, rhs, start, stop):
                return pe.matmul(o, lhsT, rhs, start=start, stop=stop, skip_group_check=True)

            def mod_chunk(l, n):
                chunk_ready(pe, l, n)
                if 12 * l + n >= 2:
                    pe.wait_ge(mod_out, 12 * l + n - 1)
                w = gu[:, slot_of(l, n)]
                if l == 0 and n < 4:
                    for k in range(KT):
                        mm(bank[:, 2 + n % 2, :], ccbc[:, k, :], w[:, k, :], k == 0, k == KT - 1)
                for k in range(KT):
                    last = mm(bank[:, n % 2, :], cbc[:, k, :], w[:, k, :], k == 0, k == KT - 1)
                last.then_inc(mod_ps, 1)

            def features(i, t):
                pe.wait_ge(nrm_h, 2 * i + t + 1)
                for g in range(2):
                    q = 2 * (2 * i + t) + g
                    if q >= 2:
                        pe.wait_ge(hT_out, q - 1)
                    for k in range(4):
                        last = pe.transpose(bank[:, 6 + g, k * P:(k + 1) * P], hh[:, t, (4 * g + k) * P:(4 * g + k + 1) * P], ident)
                    last.then_inc(hT_ps, 1)

            def project_ab():
                pe.wait_ge(mod_out, 12)
                pe.wait_ge(hT_out, 8)
                pe.wait_ge(gate_w, 1)
                for f in range(2):
                    for half, tok in enumerate((hc, hl)):
                        for k in range(KT):
                            last = mm(bank[0:64, 4 + f, half * T:(half + 1) * T], wgz[:, k, f, :], tok[:, k, :], k == 0, k == KT - 1)
                    last.then_inc(gate_ps, 1)
                u = 0
                for c, n_units in enumerate(N_AB):
                    n = 12 + c
                    chunk_ready(pe, 0, n)
                    w = gu[:, slot_of(0, n)]
                    for j in range(n_units):
                        if u >= 4:
                            pe.wait_ge(*unit_read(u - 4))
                        o = bank[:, u % 4, :]
                        if c in (0, 1):
                            for k in range(KT):
                                last = mm(o[:, 0:T], w[:, k, j * P:(j + 1) * P], hl[:, k, :], k == 0, k == KT - 1)
                        elif c in (3, 5):
                            for half, tok in enumerate((hc, hl)):
                                for k in range(KT):
                                    last = mm(o[:, half * T:(half + 1) * T], w[:, k, j * P:(j + 1) * P], tok[:, k, :], k == 0, k == KT - 1)
                        else:
                            tok = hl if c == 2 or j >= 2 else hc
                            for k in range(KT):
                                last = mm(o, tok[:, k, (j % 2) * P:(j % 2 + 1) * P], w[:, k, :], k == 0, k == KT - 1)
                        last.then_inc(proj_ps, 1)
                        u += 1

            def ropes():
                pe.wait_ge(*unit_read(13))
                for q in range(4):
                    if q == 0:
                        pe.wait_ge(gate_x, 1)
                    for j in range(2):
                        h = 2 * (q % 2) + j
                        src = qraw[:, h, :] if q < 2 else kk[:, h, T:2 * T]
                        last = mm(bank[:, 4 + q, j * T:(j + 1) * T], const(C_ROT), src, True, True)
                    last.then_inc(rot_ps, 1)

            def lambda_and_decay():
                pe.wait_ge(lam_p, 1)
                pe.wait_ge(*unit_read(25))
                pe.wait_ge(*unit_read(21))
                mm(bank[:, 3, 0:2], ones, st[:, 0:2], True, True).then_inc(lam_ps, 1)
                pe.wait_ge(crow, 1)
                mm(bank[:, 0, 0:8], ones, st[:, 8:16], True, True)
                for t in range(TT):
                    last = pe.transpose(bank[:, 1 + t, 0:P], decay_b[:, t * P:(t + 1) * P], ident)
                last.then_inc(bcol_ps, 1)

            def scores(u):
                g, h, b = u // 4, u % 4, 3 * (u % 2)
                t = g % 2
                if u == 0:
                    pe.wait_ge(rot_out, 4)
                    pe.wait_ge(bcol_out, 1)
                    pe.wait_ge(lam_e, 1)
                if u == 8:
                    pe.wait_ge(cv_out, 8)
                    pe.wait_ge(s_ab, 64)
                if u >= 2:
                    pe.wait_ge(a_ready, u - 1)
                tok = slice(t * P, (t + 1) * P)
                if g < 2:
                    for c in range(2):
                        last = mm(bank[:, b + c, :], qz[:, c, h, tok], kk[:, h, :], True, True)
                else:
                    mm(bank[:, b, :], bq[:, h, tok], bk[:, h, :], True, True)
                    for d in range(2):
                        last = mm(bank[:, b + 1 + d, :], pick[:, 4 * d + h, :], decay_c, True, True)
                last.then_inc(score_ps, 1)

            def values(u):
                g, h = u // 4, u % 4
                pe.wait_ge(a_ready, u + 1)
                if u:
                    pe.wait_ge(at_out, u)
                for j in range(4):
                    last = pe.transpose(bank[:, 6, j * P:(j + 1) * P], amat[:, u % 2, j * P:(j + 1) * P], ident)
                last.then_inc(at_ps, 1)
                pe.wait_ge(at_out, u + 1)
                if h == 0 and g:
                    pe.wait_ge(o_out, g)
                v = av if g < 2 else bv
                for j in range(4):
                    last = mm(bank[:, 7, h * DV:(h + 1) * DV], aT[:, u % 2, j * P:(j + 1) * P], v[:, j, h * DV:(h + 1) * DV],
                              j == 0, j == 3)
                last.then_inc(pv_ps, 1)

            def out_ab():
                pe.wait_ge(at_out, 16)
                pe.wait_ge(o_out, 4)
                for t in range(TT):
                    pe.wait_ge(cat_out, 4)
                    for g in range(2):
                        if t:
                            pe.wait_ge(cT_out, g + 1)
                        for k in range(4):
                            last = pe.transpose(bank[:, 6 + g, k * P:(k + 1) * P], cat[:, t, (4 * g + k) * P:(4 * g + k + 1) * P], ident)
                        last.then_inc(cT_ps, 1)
                pe.wait_ge(cT_out, 4)
                mix_out(0, hl)

            def mix_out(l, src):
                for n in range(HALVES):
                    i = chunk_index(l, "out", n)
                    chunk_ready(pe, l, i)
                    for t in range(TT):
                        for k in range(KT):
                            last = mm(bank[:, 2 * t + n, :], src[:, k, t * P:(t + 1) * P], gu[:, slot_of(l, i), k, :], k == 0, k == KT - 1)
                        last.then_inc(mix_ps, 1)

            def filters():
                pe.wait_ge(s_hy, 64)
                mm(bank[0:HIDDEN, 4, 0:T], par[:, Q_W1:Q_W1 + HIDDEN], raw3[:, 0, :], True, True).then_inc(f_ps, 1)
                pe.wait_ge(f_sin, 1)
                mm(bank[0:HIDDEN, 5, 0:T], par[:, Q_W2:Q_W2 + HIDDEN], raw3[:, 1, :], True, True).then_inc(f_ps, 1)
                pe.wait_ge(f_sin, 2)
                for u in range(8):
                    t, n = u // 4, u % 4
                    if u >= 4:
                        pe.wait_ge(ff_out, u - 3)
                    mm(bank[:, 4 + u % 4, :], raw3[:, 2, t * P:(t + 1) * P], fw3[:, n * NB:(n + 1) * NB], True, True).then_inc(ff_ps, 1)
                pe.wait_ge(ff_out, 8)
                for u in range(16):
                    f, n = u % 4, u // 4
                    if u >= 4:
                        pe.wait_ge(kf_out, u - 3)
                    for t in range(TT):
                        last = mm(bank[:, 4 + u % 4, :], dfwd[:, t, f * P:(f + 1) * P], filt[:, t, n * NB:(n + 1) * NB], t == 0, t == 1)
                    last.then_inc(kf_ps, 1)

            def hyena():
                pe.wait_ge(hT_out, 16)
                pe.wait_ge(mod_out, 24)
                for u in range(24):
                    c, j = u // 4, u % 4
                    if j == 0:
                        chunk_ready(pe, 1, 12 + c)
                    if u >= 4:
                        pe.wait_ge(up_out, u - 3)
                    for k in range(KT):
                        last = mm(bank[:, u % 4, 0:T], gu[:, slot_of(1, 12 + c), k, j * P:(j + 1) * P], hl[:, k, :], k == 0, k == KT - 1)
                    last.then_inc(up_ps, 1)
                for i in range(2):
                    if i == 0:
                        pe.wait_ge(up_out, 8)
                    for q in range(4):
                        t, g = q // 2, q % 2
                        if i:
                            pe.wait_ge(z_out, 8)
                        if q >= 2:
                            pe.wait_ge(vt_out, 4 * i + q - 1)
                        for k in range(4):
                            last = pe.transpose(bank[:, 6 + q % 2, k * P:(k + 1) * P], ut[:, 4 * g + k, t * P:(t + 1) * P], ident)
                        last.then_inc(vt_ps, 1)
                    pe.wait_ge(vt_out, 4 * (i + 1))
                    if i == 0:
                        pe.wait_ge(up_out, 24)
                        pe.wait_ge(kf_out, 16)
                    for n in range(HALVES):
                        if n or i:
                            pe.wait_ge(y_out, 2 * i + n)
                        for f in range(4):
                            for t in range(TT):
                                last = mm(bank[:, f, :], dfwd[:, t, f * P:(f + 1) * P], ztok[:, t, n * NB:(n + 1) * NB], t == 0, t == 1)
                        last.then_inc(sp_ps, 1)
                    pe.wait_ge(y_out, 2 * i + 2)
                    for c in range(8):
                        if c >= 2 or i:
                            pe.wait_ge(z_out, 8 * i + c - 1)
                        for f in range(4):
                            last = mm(bank[:, 4 + c % 2, 0:T], ys[:, f, c * P:(c + 1) * P], dinv[:, f, :], f == 0, f == 3)
                        last.then_inc(iv_ps, 1)
                pe.wait_ge(z_out, 16)
                mix_out(1, ut)

            def shared_expert(l):
                i = chunk_index(l, "sh", 0)
                w = gu[:, slot_of(l, i)]
                chunk_ready(pe, l, i)
                pe.wait_ge(hT_out, 4 * (2 if l == 0 else 4) + 4)
                for t in range(TT):
                    for k in range(KT):
                        last = mm(bank[:, 4 + t, :], hl[:, k, t * P:(t + 1) * P], w[:, k, :], k == 0, k == KT - 1)
                    last.then_inc(sh_ps, 1)

            def shared_down(l):
                pe.wait_ge(dn_in, 16 * (l + 1))
                pe.wait_ge(x_out, 4 * l + 2)
                for t in range(TT):
                    pe.wait_ge(sh_h, 2 * l + t + 1)
                    for f in range(2):
                        last = pe.transpose(bank[:, 7, f * P:(f + 1) * P], he[:, f * P:(f + 1) * P], ident)
                    last.then_inc(sh_tp, 1)
                    pe.wait_ge(sh_to, 2 * l + t + 1)
                    for n in range(HALVES):
                        for f in range(2):
                            last = mm(bank[:, 2 * t + n, :], hT[:, f, :], dn[:, 3, f, n * NB:(n + 1) * NB], f == 0, False)
                last.then_inc(sh_dn, 1)

            def route(l):
                pe.wait_ge(r_in, 32 * (l + 1))
                for t in range(TT):
                    for k in range(KT):
                        last = mm(bank[:, 6, t * E:(t + 1) * E], hl[:, k, t * P:(t + 1) * P], rw[:, k, :], k == 0, k == KT - 1)
                last.then_inc(r_ps, 1)

            def route_slots(l):
                pe.wait_ge(r_mk, l + 1)
                mm(bank[:, 6, 128:192], const(C_TRI), mk[:, 0, :], True, True)
                mm(bank[:, 6, 192:256], ones, mk[:, 0, :], True, False)
                mm(bank[:, 6, 192:256], const(C_TRI), mk[:, 1, :], False, True)
                mm(bank[0:E, 6, 256:257], mk[:, 0, :], const(C_ONES, 1), True, False)
                mm(bank[0:E, 6, 256:257], mk[:, 1, :], const(C_ONES, 1), False, True).then_inc(r_cu, 1)

            def route_over(l):
                pe.wait_ge(r_nx, l + 1)
                mm(bank[0:E, 6, 258:259], const(C_TRI, E), nx[:, 0:1], True, True)
                mm(bank[:, 6, 260:261], ones, nx[:, 0:1], True, True).then_inc(r_of, 1)
                pe.wait_ge(r_sel, l + 1)
                for j in range(4):
                    last = pe.transpose(bank[0:E, 7, j * P:(j + 1) * P], pg[:, 0:E, j], ident)
                last.then_inc(r_tp, 1)
                pe.wait_ge(r_to, l + 1)
                for j in range(4):
                    o = bank[:, 6, j * OVER:(j + 1) * OVER]
                    mm(o, pgT[:, j, :], sel[:, 0, :], True, j >= 2)
                    if j < 2:
                        mm(o, ones, sel[:, 1, :], False, True)
                mm(bank[0:1, 6, 4 * OVER:5 * OVER], const(C_E, 1), sel[:, 0, :], True, True).then_inc(r_ov, 1)

            def gather(p, ph, gb, half):
                for k in range(4 * half, 4 * half + 4):
                    o = bank[:, 4, (k % 4) * P:(k % 4 + 1) * P]
                    for t in range(TT):
                        for q in range(3):
                            last = mm(o, th[:, q, t, k * P:(k + 1) * P], ptb[:, t, :], t == 0 and q == 0, t == 1 and q == 2)
                last.then_inc(ph.g_ps, 1)

            def slots_t(ph):
                for t in range(TT):
                    last = pe.transpose(bank[:, 7, t * P:(t + 1) * P], ptg[:, t, :], ident)
                last.then_inc(ph.pT_ps, 1)

            def prologue(ph, gb):
                pe.wait_ge(ph.built, gb + 1)
                gather(0, ph, gb, 0)
                pe.wait_ge(ph.g_out, 2 * gb + 1)
                gather(0, ph, gb, 1)
                slots_t(ph)

            def pair(p, ph, gb, nb, slots, uses):
                pe.wait_ge(ph.gu_in[slots[0] // 2], uses)
                pe.wait_ge(ph.g_out, 2 * p + (2 * gb + 2))
                for k in range(KT):
                    for j, s in enumerate(slots):
                        last = mm(bank[C * j:C * (j + 1), 5, :], tg[:, k, C * j:C * (j + 1)], gu[:, s, k, :], k == 0, k == KT - 1)
                last.then_inc(ph.gu_ps, 1)
                pe.wait_ge(ph.built, p + (gb + 2))
                gather(p, ph, gb, 0)
                pe.wait_ge(ph.h, p + (nb + 1))
                pe.wait_ge(ph.pT_out, p + (gb + 1))
                for f in range(2):
                    last = pe.transpose(bank[:, 7, f * P:(f + 1) * P], he[:, f * P:(f + 1) * P], ident)
                last.then_inc(ph.hT_ps, 1)
                pe.wait_ge(ph.g_out, 2 * p + (2 * gb + 3))
                gather(p, ph, gb, 1)
                pe.wait_ge(ph.hT_out, p + (nb + 1))
                pe.wait_ge(ph.dn_in[slots[0] // 2], uses)
                for n, o in enumerate((6, 5)):
                    for f in range(2):
                        for j, s in enumerate(slots):
                            last = mm(bank[C * j:C * (j + 1), o, :], hT[:, f, C * j:C * (j + 1)], dn[:, s, f, n * NB:(n + 1) * NB], f == 0, f == 1)
                    last.then_inc(ph.y_ps, 1)
                for n in range(HALVES):
                    pe.wait_ge(ph.y_out, 2 * p + (2 * nb + n + 1))
                    for t in range(TT):
                        last = mm(bank[:, 2 * t + n, :], pm[:, t * P:(t + 1) * P], ye[:, n, :], False, False)
                slots_t(ph)

            def moe(l):
                shared_expert(l)
                route(l)
                shared_down(l)
                route_slots(l)
                route_over(l)
                pe.wait_ge(split_out, 2 * (l + 1))
                pe.wait_ge(r_id, l + 1)
                gb, nb = (PAIRS + 1) * l, PAIRS * l
                prologue(first, gb)
                with pe.Fori(0, PAIRS // 2) as i:
                    for b in range(2):
                        pair(2 * i + b, first, gb, nb, (2 * b, 2 * b + 1), 32 * i + 32 * (l * (PAIRS // 2) + 1))
                ph = further[l]
                pe.nop("credit").then_inc(ph.gu_ps, 1)
                pe.nop("credit").then_inc(ph.y_ps, 2)
                pe.wait_ge(first.g_out, 2 * (gb + PAIRS + 1))
                pe.wait_ge(first.pT_out, gb + PAIRS + 1)
                prologue(ph, 0)
                n = pe.value_load(eid[0:1, 36:37], min_val=1, max_val=OVER // 2)
                with pe.Fori(0, n) as i:
                    pair(i, ph, 0, 0, (0, 1), 32 * i + 32)
                for b in range(4):
                    last = mm(bank[:, b, 0:1], ident, st[:, 127:128], False, True)
                last.then_inc(over_free, 1)

            pe.wait_ge(s_const, 32)
            pe.wait_ge(s_cbc, 2)
            for n in range(8):
                mod_chunk(0, n)
            for i in range(2):
                for t in range(TT):
                    features(i, t)
            for n in range(8, 12):
                mod_chunk(0, n)
            project_ab()
            ropes()
            lambda_and_decay()
            scores(0)
            for u in range(16):
                if u < 15:
                    scores(u + 1)
                values(u)
            out_ab()
            for t in range(TT):
                features(2, t)
            moe(0)
            pe.wait_ge(x_out, 4)
            filters()
            for n in range(12):
                mod_chunk(1, n)
            pe.wait_ge(kf_out, 16)
            for t in range(TT):
                features(3, t)
            hyena()
            for t in range(TT):
                features(4, t)
            moe(1)

        @block.scalar
        def _(act):
            def act_fn(o, i, f, **kw):
                return nc.scalar.activation(o, i, f, **kw)

            def root(i, t):
                act.wait_ge(nrm_ms, 2 * i + t + 1)
                act_fn(st[:, 98 + 4 * t:99 + 4 * t], st[:, 97 + 4 * t:98 + 4 * t], ACT.Sqrt).then_inc(nrm_sd, 1)

            def features(i, t):
                dst = hc if i == 0 else hl
                for g in range(2):
                    act.wait_ge(hT_ps, 2 * (2 * i + t) + g + 1)
                    act_fn(dst[:, 4 * g:4 * g + 4, t * P:(t + 1) * P], bank[:, 6 + g, :].rearrange("p (k n) -> p k n", k=4),
                           ACT.Copy).then_inc(hT_out, 1)

            def units(lo, hi):
                for u in range(lo, hi):
                    act.wait_ge(proj_ps, u + 1)
                    if u == 10:
                        act.wait_ge(hT_ps, 8)
                    src = bank[:, u % 4, :]
                    if u < 4:
                        ins = act_fn(qraw[:, u, :], src[:, 0:T], ACT.Copy)
                    elif u < 10:
                        ins = act_fn(sigbo[:, u - 8, :], src, ACT.Sigmoid)
                    elif u < 14:
                        ins = act_fn(kk[:, u - 10, :], src, ACT.Copy)
                    elif u < 18:
                        ins = act_fn(av[:, u - 14, :], src, ACT.Copy)
                    else:
                        ins = act_fn(bv[:, u - 22, :], src, ACT.Copy)
                    ins.then_inc(proj_out, 1)

            def exps(u):
                g, s, b = u // 4, 40 + 16 * (u % 2), 3 * (u % 2)
                act.wait_ge(m_ready, u + 1)
                if g < 2:
                    for c in range(2):
                        act_fn(ex[:, u % 2, c, :], bank[:, b + c, :], ACT.Exp, bias=st[:, s + 2 + c:s + 3 + c], scale=DQK ** -0.5,
                               accum_out=st[:, s + 6 + c:s + 7 + c]).then_inc(e_ready, 1)
                else:
                    for d in range(2):
                        act_fn(ex[:, u % 2, d, :], ex[:, u % 2, d, :], ACT.Exp, bias=st[:, s + 2 + d:s + 3 + d]).then_inc(e_ready, 1)
                    act_fn(st[:, s + 8:s + 10], st[:, s + 4:s + 6], ACT.Exp).then_inc(e_ready, 1)

            def post_norm(j, ready, value):
                act.wait_ge(ready, value)
                for t in range(TT):
                    for n in range(HALVES):
                        act_fn(hh[:, t, n * NB:(n + 1) * NB], bank[:, 2 * t + n, :], ACT.Square,
                               accum_out=st[:, 80 + 2 * t + n:81 + 2 * t + n]).then_inc(mix_sq, 1)
                act.wait_ge(mix_ms, j + 1)
                act_fn(st[:, 88:90], st[:, 86:88], ACT.Sqrt).then_inc(mix_sd, 1)

            def first_pass(ph, p, gb, nb, c):
                act.wait_ge(ph.gu_ps, p + (nb + 1 + c))
                act_fn(sg, bank[:, 5, 0:F], ACT.Sigmoid).then_inc(ph.sig, 1)
                gathered(ph, 2 * p + (2 * gb + 3), 0)
                act.wait_ge(ph.hT_ps, p + (nb + 1))
                act_fn(hT[:, :, :].rearrange("p f n -> p (f n)"), bank[:, 7, 0:F], ACT.Copy).then_inc(ph.hT_out, 1)
                gathered(ph, 2 * p + (2 * gb + 4), 1)
                slots(ph, p + (gb + 2))

            def gathered(ph, value, half):
                act.wait_ge(ph.g_ps, value)
                act_fn(tg[:, 4 * half:4 * half + 4, :].rearrange("p k n -> p (k n)"), bank[:, 4, :], ACT.Copy).then_inc(ph.g_out, 1)

            def slots(ph, value):
                act.wait_ge(ph.pT_ps, value)
                act_fn(pm, bank[:, 7, 0:T], ACT.Copy).then_inc(ph.pT_out, 1)

            def moe(l):
                gb, nb = (PAIRS + 1) * l, PAIRS * l
                for t in range(TT):
                    act.wait_ge(sh_ps, 2 * l + t + 1)
                    if t:
                        act.wait_ge(sh_h, 2 * l + t)
                    act_fn(sg, bank[:, 4 + t, 0:F], ACT.Sigmoid).then_inc(sh_sig, 1)
                    if t == 0:
                        act.wait_ge(r_ps, l + 1)
                        act_fn(sc[:, :, :].rearrange("p t e -> p (t e)"), bank[:, 6, 0:TT * E], ACT.Sigmoid).then_inc(r_sc, 1)
                for t in range(TT):
                    act.wait_ge(sh_tp, 2 * l + t + 1)
                    act_fn(hT[:, :, :].rearrange("p f n -> p (f n)"), bank[:, 7, 0:F], ACT.Copy).then_inc(sh_to, 1)
                act.wait_ge(r_tp, l + 1)
                act_fn(pgT[0:E, :, :].rearrange("p j n -> p (j n)"), bank[0:E, 7, :], ACT.Copy).then_inc(r_to, 1)
                for half in range(2):
                    gathered(first, 2 * gb + half + 1, half)
                slots(first, gb + 1)
                with act.Fori(0, PAIRS // 2) as i:
                    for b in range(2):
                        first_pass(first, 2 * i + b, gb, nb, 0)
                ph = further[l]
                for half in range(2):
                    gathered(ph, half + 1, half)
                slots(ph, 1)
                n = act.value_load(eid[0:1, 36:37], min_val=1, max_val=OVER // 2)
                with act.Fori(0, n) as i:
                    first_pass(ph, i, 0, 0, 1)
                post_norm(2 * l + 1, over_free, l + 1)

            act.dma_start(wgr, w_in[0][:, :, 7 * NB:7 * NB + 16]).then_inc(s_wg, 16)
            act.wait_ge(s_const, 32)
            act.wait_ge(dve_step, 1)
            act_fn(st[:, 64:80], par[:, Q_C:Q_C + 16], ACT.Sigmoid).then_inc(s_silu, 1)
            for i in range(2):
                for t in range(TT):
                    root(i, t)
                for t in range(TT):
                    features(i, t)
            act.wait_ge(gate_x, 1)
            act_fn(lf, lf, ACT.Exp).then_inc(gate_e, 1)
            act.wait_ge(gate_e, 1)
            act_fn(lf, lf, ACT.Ln, bias=1.0).then_inc(gate_l, 1)
            units(0, 4)
            for u in range(HEADS):
                act.wait_ge(cv_y, u + 1)
                act_fn(sgq[:, u, :], bq[:, u, :], ACT.Sigmoid).then_inc(cv_s, 1)
            units(8, 18)
            units(22, 26)
            for u in range(HEADS):
                act.wait_ge(cv_y, u + 5)
                act_fn(sgk[:, u, :], bk[:, u, :], ACT.Sigmoid).then_inc(cv_s, 1)
            act.wait_ge(lam_ps, 1)
            act_fn(st[:, 2:4], bank[:, 3, 0:2], ACT.Exp).then_inc(lam_e, 1)
            exps(0)
            for u in range(16):
                if u < 15:
                    exps(u + 1)
                act.wait_ge(at_ps, u + 1)
                if u >= 2:
                    act.wait_ge(pv_ps, u - 1)
                act_fn(aT[:, u % 2, :], bank[:, 6, :], ACT.Copy).then_inc(at_out, 1)
                if u % 4 == 3:
                    act.wait_ge(pv_ps, u + 1)
                    act_fn(og[:, u // 4, :], bank[:, 7, :], ACT.Copy).then_inc(o_out, 1)
            for g in range(4):
                act.wait_ge(hn_ms, g + 1)
                act_fn(st[:, 112:116], st[:, 108:112], ACT.Sqrt).then_inc(hn_sd, 1)
            for t in range(TT):
                for g in range(2):
                    act.wait_ge(cT_ps, 2 * t + g + 1)
                    act_fn(hl[:, 4 * g:4 * g + 4, t * P:(t + 1) * P], bank[:, 6 + g, :].rearrange("p (k n) -> p k n", k=4),
                           ACT.Copy).then_inc(cT_out, 1)
            post_norm(0, mix_ps, 4)
            for t in range(TT):
                root(2, t)
            for t in range(TT):
                features(2, t)
            moe(0)
            for i in range(2):
                act.wait_ge(f_arg, i + 1)
                act_fn(raw3[0:HIDDEN, 1 + i, :], raw3[0:HIDDEN, 3, :], ACT.Sin).then_inc(f_sin, 1)
            for u in range(16):
                act.wait_ge(kf_ps, u + 1)
                act_fn(kf[:, u % 4, (u // 4) * NB:(u // 4 + 1) * NB], bank[:, 4 + u % 4, :], ACT.Copy).then_inc(kf_out, 1)
            for t in range(TT):
                root(3, t)
            for t in range(TT):
                features(3, t)
            for i in range(2):
                for q in range(4):
                    t, g = q // 2, q % 2
                    act.wait_ge(vt_ps, 4 * i + q + 1)
                    act_fn(ztok[:, t, g * NB:(g + 1) * NB], bank[:, 6 + g, :], ACT.Copy).then_inc(vt_out, 1)
            post_norm(2, mix_ps, 8)
            for t in range(TT):
                root(4, t)
            for t in range(TT):
                features(4, t)
            moe(1)

        @block.vector
        def _(dve):
            steps = [0]
            v = nc.vector

            def step(ins):
                steps[0] += 1
                ins.then_inc(dve_step, 1)
                dve.wait_ge(dve_step, steps[0])

            rows = [0]

            def mod_chunk(l, n):
                dve.wait_ge(mod_ps, 12 * l + n + 1)
                m, half = n // 2, slice((n % 2) * NB, (n % 2 + 1) * NB)
                rows[0] += 1 if m in (0, 3) else 2
                dve.wait_ge(s_bn, 16 * rows[0])
                outs = [(mod[:, m, half], bank[:, n % 2, :])]
                if l == 0 and n < 4:
                    outs.insert(0, (modc[:, m, half], bank[:, 2 + n % 2, :]))
                for o, src in outs:
                    ins = v.tensor_tensor(o, src, bn[:, 0, :], ALU.add)
                    if m in (1, 4):
                        step(ins)
                        ins = v.scalar_tensor_tensor(o, o, 1.0, bn[:, 1, :], ALU.add, ALU.mult)
                    elif m in (2, 5):
                        step(ins)
                        ins = v.tensor_tensor(o, o, bn[:, 1, :], ALU.mult)
                    if o is not outs[-1][0]:
                        step(ins)
                ins.then_inc(mod_out, 1)

            def norm(i, t):
                src = (cx if i == 0 else x)[:, t, :]
                table = modc if i == 0 else mod
                m = 3 if i in (2, 4) else 0
                s = 96 + 4 * t
                if i:
                    dve.wait_ge(hT_ps, 2 * (2 * (i - 1) + t + 1))
                step(v.tensor_tensor_reduce(hh[:, t, :], src, src, 1.0, 0.0, ALU.mult, ALU.add, st[:, s:s + 1]))
                v.tensor_scalar(st[:, s + 1:s + 2], st[:, s:s + 1], 1.0 / D, EPS, ALU.mult, ALU.add).then_inc(nrm_ms, 1)
                dve.wait_ge(nrm_sd, 2 * i + t + 1)
                step(v.reciprocal(st[:, s + 3:s + 4], st[:, s + 2:s + 3]))
                step(v.scalar_tensor_tensor(hh[:, t, :], src, st[:, s + 3:s + 4], table[:, m + 1, :], ALU.mult, ALU.mult))
                v.tensor_tensor(hh[:, t, :], hh[:, t, :], table[:, m, :], ALU.add).then_inc(nrm_h, 1)

            def post_norm(j):
                l, m = j // 2, 5 if j % 2 else 2
                dve.wait_ge(mix_sq, 4 * (j + 1))
                sq = st[:, 80:84].rearrange("p (t n) -> p t n", t=TT)
                step(v.tensor_tensor(st[:, 84:86], sq[:, :, 0], sq[:, :, 1], ALU.add))
                v.tensor_scalar(st[:, 86:88], st[:, 84:86], 1.0 / D, EPS, ALU.mult, ALU.add).then_inc(mix_ms, 1)
                dve.wait_ge(mix_sd, j + 1)
                step(v.reciprocal(st[:, 90:92], st[:, 88:90]))
                for t in range(TT):
                    for n in range(HALVES):
                        half = slice(n * NB, (n + 1) * NB)
                        step(v.scalar_tensor_tensor(hh[:, t, half], bank[:, 2 * t + n, :], st[:, 90 + t:91 + t], mod[:, m, half],
                                                    ALU.mult, ALU.mult))
                    v.tensor_tensor(x[:, t, :], x[:, t, :], hh[:, t, :], ALU.add).then_inc(x_out, 1)
                dve.wait_ge(x_out, 2 * (j + 1))

            def taps(o, src, w, b, segs):
                step(v.tensor_scalar(o, src, w[1], b, ALU.mult, ALU.add))
                for s0, s1 in segs:
                    step(v.scalar_tensor_tensor(o[:, s0 + 1:s1], src[:, s0:s1 - 1], w[0], o[:, s0 + 1:s1], ALU.mult, ALU.add))
                for s0, s1 in segs:
                    ins = v.scalar_tensor_tensor(o[:, s0:s1 - 1], src[:, s0 + 1:s1], w[2], o[:, s0:s1 - 1], ALU.mult, ALU.add)
                    if (s0, s1) != segs[-1]:
                        step(ins)
                return ins

            def pcol(c):
                return par[:, c:c + 1]

            def conv_ab(u, o):
                dve.wait_ge(proj_ps, (u + 5) if u < 4 else (u + 15))
                unit = u + 4 if u < 4 else u + 14
                segs = [(0, T)] if u < 4 else [(0, T), (T, 2 * T)]
                w = [pcol(Q_CAW + 8 * j + u) for j in range(3)]
                taps(o, bank[:, unit % 4, 0:segs[-1][1]], w, pcol(Q_CAB + u), segs).then_inc(cv_y, 1)

            def conv_gate(u, o, s):
                dve.wait_ge(cv_s, u + 1)
                v.scalar_tensor_tensor(o, o, DV ** -0.5 if u < 4 else 1.0, s, ALU.mult, ALU.mult).then_inc(cv_out, 1)

            def decay_rows():
                dve.wait_ge(gate_l, 1)
                step(v.scalar_tensor_tensor(lf, fg, 0.0, lf, ALU.min, ALU.subtract))
                for s in range(2):
                    seg = slice(s * T, (s + 1) * T)
                    step(v.tensor_tensor_scan(pre[:, seg], small[0:64, C_ONES:C_ONES + T], lf[:, seg], 0.0, ALU.mult, ALU.add))
                ctx_, lat = slice(0, T), slice(T, 2 * T)
                fw, bw = slice(0, 32), slice(32, 64)
                tc, tl = pre[:, T - 1:T], pre[:, 2 * T - 1:2 * T]
                step(v.scalar_tensor_tensor(decay_c[fw, :], pre[fw, :], -1.0, ig[fw, :], ALU.mult, ALU.add))
                step(v.tensor_scalar(decay_c[fw, ctx_], decay_c[fw, ctx_], tc[fw], None, ALU.add))
                step(v.tensor_copy(decay_b[fw, :], pre[fw, lat]))
                step(v.tensor_tensor(fg[bw, :], pre[bw, :], lf[bw, :], ALU.subtract))
                step(v.tensor_tensor(decay_c[bw, :], ig[bw, :], fg[bw, :], ALU.add))
                step(v.tensor_scalar(decay_c[bw, lat], decay_c[bw, lat], tl[bw], None, ALU.subtract))
                step(v.tensor_scalar(decay_b[bw, :], fg[bw, lat], -1.0, tl[bw], ALU.mult, ALU.add))
                v.tensor_scalar(st[0:64, 8:16], small[0:64, C_ROW8:C_ROW8 + 8], tc, None, ALU.mult).then_inc(crow, 1)

            def stats(u):
                s = 40 + 16 * (u % 2)
                return [st[:, s + 2 * i:s + 2 * i + 2] for i in range(8)]

            def maxima(u):
                g, h, b = u // 4, u % 4, 3 * (u % 2)
                mx, neg, nmt = stats(u)[0:3]
                dve.wait_ge(score_ps, u + 1)
                if g < 2:
                    for c in range(2):
                        step(v.tensor_reduce(mx[:, c:c + 1], bank[:, b + c, :], AX_X, ALU.max))
                    v.tensor_scalar(neg, mx, -DQK ** -0.5, None, ALU.mult).then_inc(m_ready, 1)
                else:
                    if u == 8:
                        dve.wait_ge(s_ab, 64)
                    for d in range(2):
                        step(v.tensor_tensor_reduce(ex[:, u % 2, d, :], bank[:, b + 1 + d, :], mask[:, d, g % 2, :], 1.0,
                                                    st[:, 16 + 4 * d + h:17 + 4 * d + h], ALU.add, ALU.max, mx[:, d:d + 1]))
                    step(v.tensor_scalar(neg, mx, -1.0, None, ALU.mult))
                    bcols = st[:, 24 + 8 * (g % 2):32 + 8 * (g % 2)].rearrange("p (d h) -> p d h", d=2)[:, :, h]
                    v.tensor_tensor(nmt, neg, bcols, ALU.subtract).then_inc(m_ready, 1)

            def weights(u):
                g, b = u // 4, 3 * (u % 2)
                _, _, _, sm, en, r = stats(u)[0:6]
                e, o = ex[:, u % 2], amat[:, u % 2, :]
                dve.wait_ge(e_ready, 2 * (u + 1) if u < 8 else 16 + 3 * (u - 7))
                if g < 2:
                    step(v.reciprocal(r, sm))
                    step(v.tensor_scalar(r[:, 1:2], r[:, 1:2], st[:, 5:6], None, ALU.mult))
                else:
                    for d in range(2):
                        step(v.tensor_tensor_reduce(e[:, d, :], bank[:, b, :], e[:, d, :], 1.0, 0.0, ALU.mult, ALU.add,
                                                    sm[:, d:d + 1]))
                    step(v.scalar_tensor_tensor(sm, sm, -1.0, sm, ALU.mult, ALU.max))
                    step(v.tensor_tensor(sm, sm, en, ALU.max))
                    step(v.reciprocal(r, sm))
                if u >= 2:
                    dve.wait_ge(at_ps, u - 1)
                step(v.tensor_scalar(o, e[:, 0, :], r[:, 0:1], None, ALU.mult))
                v.scalar_tensor_tensor(o, e[:, 1, :], r[:, 1:2], o, ALU.mult, ALU.add).then_inc(a_ready, 1)

            def head_norm(g):
                t, half = g % 2, slice((g // 2) * NB, (g // 2 + 1) * NB)
                dve.wait_ge(o_out, g + 1)
                o = cat[:, t, half]
                for h in range(HEADS):
                    src = og[:, g, h * DV:(h + 1) * DV]
                    step(v.tensor_tensor_reduce(o[:, h * DV:(h + 1) * DV], src, src, 1.0, 0.0, ALU.mult, ALU.add,
                                                st[:, 104 + h:105 + h]))
                v.tensor_scalar(st[:, 108:112], st[:, 104:108], 1.0 / DV, EPS, ALU.mult, ALU.add).then_inc(hn_ms, 1)
                dve.wait_ge(hn_sd, g + 1)
                step(v.reciprocal(st[:, 116:120], st[:, 112:116]))
                step(v.tensor_tensor(o.rearrange("p (h n) -> p h n", h=HEADS), og[:, g, :].rearrange("p (h n) -> p h n", h=HEADS),
                                     st[:, 116:120].unsqueeze(2).broadcast_to([P, HEADS, DV]), ALU.mult))
                ins = v.tensor_tensor(o, o, hgain[:, g // 2, :], ALU.mult)
                if g >= 2:
                    step(ins)
                    ins = v.tensor_tensor(o, o, sigbo[:, t, :], ALU.mult)
                ins.then_inc(cat_out, 1)

            def filters():
                step(v.memset(raw3[:, 1:3, :], 0.0))
                turns = raw3[0:HIDDEN, 4, :]
                whole = raw3[0:HIDDEN, 5, :].bitcast(I32)
                arg = raw3[0:HIDDEN, 3, :]
                for i in range(2):
                    dve.wait_ge(f_ps, i + 1)
                    step(v.tensor_scalar(arg, bank[0:HIDDEN, 4 + i, 0:T], par[0:HIDDEN, Q_B + i:Q_B + i + 1], None, ALU.add))
                    step(v.tensor_scalar(whole, arg, 1.0 / (2 * math.pi), None, ALU.mult))
                    step(v.tensor_copy(turns, whole))
                    high = 6.28125
                    step(v.scalar_tensor_tensor(arg, turns, -high, arg, ALU.mult, ALU.add))
                    step(v.scalar_tensor_tensor(arg, turns, -(2 * math.pi - high), arg, ALU.mult, ALU.add))
                    v.tensor_scalar(arg, arg, 3.1415925, -3.1415925, ALU.min, ALU.max).then_inc(f_arg, 1)
                    dve.wait_ge(f_sin, i + 1)
                dve.wait_ge(s_hy, 64)
                for u in range(8):
                    t, n = u // 4, u % 4
                    dve.wait_ge(ff_ps, u + 1)
                    v.tensor_tensor(filt[:, t, n * NB:(n + 1) * NB], bank[:, 4 + u % 4, :], window[:, t, (n % 2) * NB:(n % 2 + 1) * NB],
                                    ALU.mult).then_inc(ff_out, 1)

            def hyena():
                for u in range(24):
                    dve.wait_ge(up_ps, u + 1)
                    w = [pcol(Q_CHW + 24 * j + u) for j in range(3)]
                    taps(ut[:, u, :], bank[:, u % 4, 0:T], w, pcol(Q_CHB + u), [(0, T)]).then_inc(up_out, 1)
                dve.wait_ge(up_out, 24)
                tmp = [hl[:, 2 * j:2 * j + 2, :].rearrange("p k t -> p (k t)") for j in range(2)]
                for i in range(2):
                    for n in range(HALVES):
                        dve.wait_ge(sp_ps, 2 * i + n + 1)
                        half = slice(n * NB, (n + 1) * NB)
                        for j in range(2):
                            re, im = bank[:, j, :], bank[:, 2 + j, :]
                            kr = kf[:, j, i * D + n * NB:i * D + (n + 1) * NB]
                            ki = kf[:, 2 + j, i * D + n * NB:i * D + (n + 1) * NB]
                            v.tensor_tensor(ys[:, j, half], re, kr, ALU.mult)
                            v.tensor_tensor(tmp[0], im, ki, ALU.mult)
                            v.tensor_tensor(ys[:, 2 + j, half], re, ki, ALU.mult)
                            step(v.tensor_tensor(tmp[1], im, kr, ALU.mult))
                            v.tensor_tensor(ys[:, j, half], ys[:, j, half], tmp[0], ALU.subtract)
                            ins = v.tensor_tensor(ys[:, 2 + j, half], ys[:, 2 + j, half], tmp[1], ALU.add)
                            if j == 0:
                                step(ins)
                        ins.then_inc(y_out, 1)
                    for c in range(8):
                        dve.wait_ge(iv_ps, 8 * i + c + 1)
                        step(v.scalar_tensor_tensor(ut[:, c, :], ut[:, c, :], pcol(Q_FB + 8 * i + c), bank[:, 4 + c % 2, 0:T],
                                                    ALU.mult, ALU.add))
                        v.tensor_tensor(ut[:, c, :], ut[:, c, :], ut[:, 8 * (i + 1) + c, :], ALU.mult).then_inc(z_out, 1)
                    dve.wait_ge(z_out, 8 * (i + 1))

            def shared(l):
                for t in range(TT):
                    dve.wait_ge(sh_sig, 2 * l + t + 1)
                    if t:
                        dve.wait_ge(sh_tp, 2 * l + t)
                    step(v.tensor_tensor(he, sg, bank[:, 4 + t, 0:F], ALU.mult))
                    v.tensor_tensor(he, he, bank[:, 4 + t, F:2 * F], ALU.mult).then_inc(sh_h, 1)

            def route(l):
                v.memset(pg[:, E:E + 4, :], 0.0)
                v.memset(pgo[:, OVER:OVER + 4, :], 0.0)
                step(v.memset(over_tiles, 0.0))
                step(v.memset(g12[:, :, 8:12], BIG))
                dve.wait_ge(r_in, 32 * (l + 1))
                dve.wait_ge(r_sc, l + 1)
                step(v.tensor_tensor(bi, sc, rb.unsqueeze(1).broadcast_to([P, TT, E]), ALU.add))
                for t in range(TT):
                    for g in range(NG):
                        ins = v.max(m8[:, t, g, :], bi[:, t, 8 * g:8 * g + 8])
                step(ins)
                step(v.tensor_tensor(g12[:, :, 0:8], m8[:, :, :, 0], m8[:, :, :, 1], ALU.add))
                for t in range(TT):
                    step(v.max(top[:, t, :], g12[:, t, :]))
                    step(v.match_replace(g12r[:, t, :], top[:, t, :], g12[:, t, :], -BIG))
                step(v.tensor_tensor(gm, g12r[:, :, 0:8], g12[:, :, 0:8], ALU.not_equal))
                step(v.tensor_scalar(gm, gm, 1.0, BIG, ALU.subtract, ALU.mult))
                step(v.tensor_tensor(bi.rearrange("p t (g e) -> p (t g) e", g=NG), bi.rearrange("p t (g e) -> p (t g) e", g=NG),
                                     gm.rearrange("p t g -> p (t g)").unsqueeze(2).broadcast_to([P, TT * NG, 8]), ALU.add))
                for t in range(TT):
                    step(v.max(top[:, t, :], bi[:, t, :]))
                    step(v.match_replace(mk[:, t, :], top[:, t, :], bi[:, t, :], -3e38))
                v.tensor_tensor(mk, mk, bi, ALU.not_equal).then_inc(r_mk, 1)
                dve.wait_ge(r_mk, l + 1)
                step(v.tensor_tensor(sc, sc, mk, ALU.mult))
                step(v.tensor_reduce(nx[:, 2:4], sc, AX_X, ALU.add))
                step(v.reciprocal(nx[:, 2:4], nx[:, 2:4]))
                step(v.tensor_scalar(nx[:, 2:4], nx[:, 2:4], 2.5, None, ALU.mult))
                for t in range(TT):
                    v.tensor_scalar(pg[:, 0:E, 2 + t], sc[:, t, :], nx[:, 2 + t:3 + t], None, ALU.mult)
                dve.wait_ge(r_cu, l + 1)
                for t in range(TT):
                    ins = v.tensor_tensor(pg[:, 0:E, t], bank[:, 6, 128 + t * E:128 + (t + 1) * E], mk[:, t, :], ALU.mult)
                ins.then_inc(r_pg, 1)
                cnt = bank[0:E, 6, 256:257]
                step(v.tensor_scalar(nx[0:E, 0:1], cnt, float(C), None, ALU.is_gt))
                for q in (2, 3):
                    step(v.tensor_scalar(nx[0:E, 1:2], cnt, float(q * C), None, ALU.is_gt))
                    ins = v.tensor_tensor(nx[0:E, 0:1], nx[0:E, 0:1], nx[0:E, 1:2], ALU.add)
                    if q == 2:
                        step(ins)
                ins.then_inc(r_nx, 1)
                dve.wait_ge(r_of, l + 1)
                end, total = bank[0:E, 6, 258:259], bank[0:1, 6, 260:261]
                step(v.tensor_tensor(nx[0:E, 1:2], end, nx[0:E, 0:1], ALU.subtract))
                kcol = small[0:E, C_K:C_K + OVER]
                step(v.tensor_scalar(sel[0:E, 1, :], kcol, end, None, ALU.is_ge))
                step(v.tensor_scalar(sel[0:E, 0, :], kcol, nx[0:E, 1:2], None, ALU.is_ge))
                step(v.tensor_tensor(sel[0:E, 0, :], sel[0:E, 0, :], sel[0:E, 1, :], ALU.subtract))
                step(v.tensor_scalar(sel[0:E, 1, :], kcol, nx[0:E, 1:2], 1.0, ALU.subtract, ALU.add))
                step(v.scalar_tensor_tensor(sel[0:E, 1, :], sel[0:E, 1, :], -float(C), sel[0:E, 0, :], ALU.mult, ALU.mult))
                step(v.tensor_scalar(nx[0:1, 1:2], total, 0.5, 0.25, ALU.mult, ALU.add))
                v.tensor_scalar(nx[0:1, 1:2], nx[0:1, 1:2], 1.0, None, ALU.max).then_inc(r_sel, 1)
                dve.wait_ge(r_sel, l + 1)
                dve.wait_ge(r_ov, l + 1)
                for j in range(4):
                    v.tensor_copy(pgo[:, 0:OVER, j], bank[:, 6, j * OVER:(j + 1) * OVER])
                step(v.memset(eid, 0))
                v.tensor_copy(eid[0:1, 36:37], nx[0:1, 1:2])
                v.tensor_copy(eid[0:1, 0:OVER], bank[0:1, 6, 4 * OVER:5 * OVER]).then_inc(r_id, 1)

            def build_slots(table, p, ph, gb):
                v.tensor_copy(pgc[:, :, :].rearrange("p j c -> p (j c)"),
                              table[:, bass.ds(2 * p, 2), :].rearrange("p j c -> p (j c)")).then_inc(ph.step, 1)
                dve.wait_ge(ph.step, p + (gb + 1))
                for t in range(TT):
                    v.tensor_tensor(ptb[:, t, :].rearrange("p (j s) -> p j s", j=2), const(C_SLOT, C).unsqueeze(1).broadcast_to([P, 2, C]),
                                    pgc[:, :, t:t + 1].broadcast_to([P, 2, C]), ALU.is_equal)
                for t in range(TT):
                    for j in range(2):
                        last = v.tensor_scalar(ptg[:, t, C * j:C * (j + 1)], const(C_SLOT, C), pgc[:, j, t:t + 1],
                                               pgc[:, j, 2 + t:3 + t], ALU.is_equal, ALU.mult)
                last.then_inc(ph.built, 1)

            def pair(ph, p, nb, gb, c, table):
                dve.wait_ge(ph.g_ps, 2 * p + (2 * gb + 2))
                dve.wait_ge(ph.pT_ps, p + (gb + 1))
                build_slots(table, p + 1, ph, gb)
                dve.wait_ge(ph.gu_ps, p + (nb + 1 + c))
                dve.wait_ge(ph.sig, p + (nb + 1))
                v.tensor_tensor(he, sg, bank[:, 5, 0:F], ALU.mult).then_inc(ph.hs, 1)
                dve.wait_ge(ph.hs, p + (nb + 1))
                v.tensor_tensor(he, he, bank[:, 5, F:2 * F], ALU.mult).then_inc(ph.h, 1)
                for n, o in enumerate((6, 5)):
                    dve.wait_ge(ph.y_ps, 2 * p + (2 * nb + n + 1 + 2 * c))
                    v.tensor_copy(ye[:, n, :], bank[:, o, :]).then_inc(ph.y_out, 1)

            def moe(l):
                route(l)
                gb = (PAIRS + 1) * l
                build_slots(pg, 0, first, gb)
                with dve.Fori(0, PAIRS // 2) as i:
                    for b in range(2):
                        pair(first, 2 * i + b, PAIRS * l, gb, 0, pg)
                dve.wait_ge(first.g_ps, 2 * (gb + PAIRS + 1))
                dve.wait_ge(first.pT_ps, gb + PAIRS + 1)
                build_slots(pgo, 0, further[l], 0)
                n = dve.value_load(eid[0:1, 36:37], min_val=1, max_val=OVER // 2)
                with dve.Fori(0, n) as i:
                    pair(further[l], i, 0, 0, 1, pgo)
                post_norm(2 * l + 1)

            step(v.memset(st[:, :], 0.0))
            dve.wait_ge(s_silu, 1)
            step(v.tensor_tensor(st[:, 64:80], st[:, 64:80], par[:, Q_C:Q_C + 16], ALU.mult))
            v.tensor_copy(cbc[:, :, :], st[:, 64:72].unsqueeze(2).broadcast_to([P, KT, P])).then_inc(s_cbc, 1)
            v.tensor_copy(ccbc, st[:, 72:80].unsqueeze(2).broadcast_to([P, KT, P])).then_inc(s_cbc, 1)
            dve.wait_ge(s_wg, 16)
            step(v.memset(wgz, 0.0))
            for f in range(2):
                for d in range(2):
                    ins = v.tensor_copy(wgz[:, :, f, 32 * d:32 * d + 4], wgr[:, :, 8 * d + 4 * f:8 * d + 4 * f + 4])
            ins.then_inc(gate_w, 1)
            for n in range(4):
                mod_chunk(0, n)
            dve.wait_ge(mod_out, 4)
            dve.wait_ge(s_tok, 32)
            for q in range(4):
                norm(q // 2, q % 2)
                mod_chunk(0, 4 + q)
            for n in range(8, 12):
                mod_chunk(0, n)
            dve.wait_ge(mod_out, 12)
            step(v.memset(bnf, 0.0))
            dve.wait_ge(gate_ps, 2)
            step(v.tensor_scalar(ig, bank[0:64, 4, :], par[0:64, Q_GB:Q_GB + 1], None, ALU.add))
            step(v.tensor_scalar(fg, bank[0:64, 5, :], par[0:64, Q_GB + 1:Q_GB + 2], None, ALU.add))
            v.scalar_tensor_tensor(lf, fg, -1.0, fg, ALU.mult, ALU.min).then_inc(gate_x, 1)
            decay_rows()
            for u in range(HEADS):
                conv_ab(u, bq[:, u, :])
            for u in range(HEADS):
                conv_gate(u, bq[:, u, :], sgq[:, u, :])
            for u in range(HEADS):
                conv_ab(4 + u, bk[:, u, :])
            for u in range(HEADS):
                conv_gate(4 + u, bk[:, u, :], sgk[:, u, :])
            dve.wait_ge(cv_out, 8)
            dve.wait_ge(s_zero, 1)
            for q in range(4):
                dve.wait_ge(rot_ps, q + 1)
                hs = slice(2 * (q % 2), 2 * (q % 2) + 2)
                src = qraw[:, hs, :] if q < 2 else kk[:, hs, T:2 * T]
                two = [P, 2, T]
                step(v.tensor_tensor(rope, bank[:, 4 + q, :].rearrange("p (j t) -> p j t", j=2), sin.unsqueeze(1).broadcast_to(two), ALU.mult))
                step(v.tensor_tensor(src, src, cos.unsqueeze(1).broadcast_to(two), ALU.mult))
                if q < 2:
                    step(v.tensor_tensor(qz[0:64, 0, hs, :], src[0:64], rope[0:64], ALU.add))
                    v.tensor_tensor(qz[64:128, 1, hs, :], src[64:128], rope[64:128], ALU.add).then_inc(rot_out, 1)
                else:
                    v.tensor_tensor(src, src, rope, ALU.add).then_inc(rot_out, 1)
                dve.wait_ge(rot_out, q + 1)
            lv = par[:, Q_LV:Q_LV + 4].rearrange("p (a b) -> p a b", a=2)
            v.tensor_tensor(st[:, 0:2], lv[:, :, 0], lv[:, :, 1], ALU.mult).then_inc(lam_p, 1)
            dve.wait_ge(lam_e, 1)
            step(v.tensor_tensor(st[:, 4:5], st[:, 3:4], st[:, 2:3], ALU.subtract))
            step(v.tensor_scalar(st[:, 5:6], st[:, 4:5], LAM_INIT, None, ALU.subtract))
            dve.wait_ge(bcol_ps, 1)
            step(v.tensor_copy(st[:, 16:24], bank[:, 0, 0:8]))
            for t in range(TT):
                ins = v.tensor_copy(st[:, 24 + 8 * t:32 + 8 * t].rearrange("p (d h) -> p d h", d=2),
                                    bank[:, 1 + t, 0:64].rearrange("p (d r) -> p d r", d=2)[:, :, 0:4])
                if t == 0:
                    step(ins)
            ins.then_inc(bcol_out, 1)
            dve.wait_ge(bcol_out, 1)
            maxima(0)
            for u in range(16):
                if u < 15:
                    maxima(u + 1)
                weights(u)
            step(v.tensor_scalar(hgain[:, 0, :], hgain[:, 0, :], 1.0 - LAM_INIT, None, ALU.mult))
            for g in range(4):
                head_norm(g)
            post_norm(0)
            for t in range(TT):
                norm(2, t)
            shared(0)
            moe(0)
            filters()
            for n in range(12):
                mod_chunk(1, n)
            dve.wait_ge(mod_out, 24)
            for t in range(TT):
                norm(3, t)
            hyena()
            post_norm(2)
            for t in range(TT):
                norm(4, t)
            shared(1)
            moe(1)


def _columns(a):
    return a.reshape(-1, P).T


def _rows(a):
    out = np.zeros((P,) + a.shape[1:], a.dtype)
    out[:a.shape[0]] = a
    return out


_LARGE = ["x", "ctx", "w_mod", "b_mod", "norm_g", "w_in_ab", "head_g_a", "head_g_b", "w_out_ab", "w_in_hy",
          "w_out_hy", "router_w", "router_b", "exp_gu", "exp_down", "sh_gu", "sh_down"]


def kernel(**inputs):
    import concourse.bacc as _bacc
    from concourse.bass_utils import run_bass_kernel_spmd as _run

    a = {k: np.asarray(v) for k, v in inputs.items()}
    arrays = {name: np.ascontiguousarray(a[name]) for name in _LARGE}
    gates = np.zeros((P, 2), np.float32)
    gb = a["gate_b_ab"][0].reshape(2, 2, HEADS)
    for d in range(2):
        gates[32 * d:32 * d + HEADS] = gb[d].T
    cols = [_columns(a["c"][0]), _columns(a["c_ctx"])]
    cols += [np.concatenate([_columns(a["conv_ab_w"][0, j]) for j in range(3)], 1), _columns(a["conv_ab_b"][0])]
    cols += [np.concatenate([_columns(a["conv_hy_w"][0, j]) for j in range(3)], 1), _columns(a["conv_hy_b"][0])]
    cols += [_columns(a["filt_bias"][0].reshape(-1)), gates, _rows(a["diff_lambda"][0].T)]
    cols += [_rows(a["filt_w1"][0]), _rows(a["filt_w2"][0]), _rows(a["filt_b1"][0][:, None]),
             _rows(a["filt_b2"][0][:, None])]
    arrays["params"] = np.ascontiguousarray(np.concatenate(cols, 1))
    arrays["filt_w3"] = _rows(a["filt_w3"][0])
    arrays.update(shape_constants())
    nc = _bacc.Bacc("TRN2", target_bir_lowering=False, num_devices=1)
    args = {n: nc.dram_tensor(f"in_{n}", v.shape, mybir.dt.from_np(v.dtype), kind="ExternalInput").ap()
            for n, v in arrays.items()}
    out = nc.dram_tensor("out_dram", (1, T, D), F32, kind="ExternalOutput").ap()
    build(nc, args, out)
    r = _run(nc, [{f"in_{n}": v for n, v in arrays.items()}], core_ids=[0])
    return r.results[0]["out_dram"]
```

```python
import concourse.bass as bass
from concourse import mybir
from contextlib import ExitStack
import math
import numpy as np

F32 = mybir.dt.float32
BF16 = mybir.dt.bfloat16
I32 = mybir.dt.int32
ALU = mybir.AluOpType
ACT = mybir.ActivationFunctionType
AX_X = mybir.AxisListType.X

P = 128
D = 1024
KT = D // P
T = 256
TT = T // P
NB = 512
HALVES = D // NB
HEADS = 4
DQK = 64
DV = 128
POS_DIM, HIDDEN = 33, 64
E = 64
NG = 8
F = 256
C = 64
OVER = 32
PAIRS = E // 2
FREQ = 256
EPS = 1e-6
LAM_INIT = 0.2
BIG = 1e30

C_IDENT, C_ROT, C_TRI, C_ONES = 0, 128, 256, 384
C_COS, C_SIN = 640, 896
C_SLOT, C_K, C_E, C_ROW8, C_END = 1152, 1216, 1248, 1249, 1257
Q_C, Q_CC = 0, 8
Q_CAW, Q_CAB = 16, 40
Q_CHW, Q_CHB = 48, 120
Q_FB, Q_GB, Q_LV = 144, 160, 161
Q_W1, Q_W2, Q_B = 165, 229, 293
Q_END = 295


def shape_constants():
    small = np.zeros((P, C_END), np.float32)
    small[:, C_IDENT:C_IDENT + P] = np.eye(P)
    for m in range(P):
        low = m % 32 < 16
        small[m + 16 if low else m - 16, C_ROT + m] = -1.0 if low else 1.0
    small[:, C_TRI:C_TRI + P] = np.triu(np.ones((P, P)))
    small[:, C_ONES:C_ONES + T] = 1.0
    pairs = DQK // 4
    inv = (np.float32(10000.0) ** (-np.arange(pairs, dtype=np.float32) / pairs)).astype(np.float32)
    tok = np.arange(T)
    place = np.stack([tok // 64, tok % 64], -1).astype(np.float32)
    ang = place[..., None] * inv
    ang = np.broadcast_to(ang[:, :, None, :], (T, 2, 2, pairs)).reshape(T, DQK)
    small[:, C_COS:C_COS + T] = np.tile(np.cos(ang).T, (2, 1))
    small[:, C_SIN:C_SIN + T] = np.tile(np.sin(ang).T, (2, 1))
    small[:, C_SLOT:C_SLOT + C] = np.arange(1, C + 1)
    small[:, C_K:C_K + OVER] = np.arange(OVER)
    small[:, C_E] = np.arange(P)
    rows = [32 * d + h for d in range(2) for h in range(HEADS)]
    for r, row in enumerate(rows):
        small[row, C_ROW8 + r] = 1.0
    pick = np.zeros((P, 8, P), np.float32)
    for r, row in enumerate(rows):
        pick[row, r, :] = 1.0
    mask = np.zeros((P, 2, TT, 2 * T), np.float32)
    t = np.arange(T).reshape(TT, P).T[:, :, None]
    s = np.arange(T)[None, None, :]
    mask[:, 0, :, T:] = np.where(s <= t, 0.0, -BIG)
    mask[:, 1, :, T:] = np.where(s >= t, 0.0, -BIG)
    w = 2 * np.pi * (np.arange(FREQ) + 0.5) / (2 * FREQ)
    fwd = np.concatenate([np.cos(np.outer(np.arange(T), w)), -np.sin(np.outer(np.arange(T), w))], 1)
    fwd = fwd.reshape(TT, P, 2 * FREQ).transpose(1, 0, 2)
    late = np.arange(T) + T // 2
    inv_ = np.concatenate([np.cos(np.outer(w, late)), -np.sin(np.outer(w, late))], 0) / FREQ
    inv_ = inv_.reshape(4, P, T).transpose(1, 0, 2)
    dft = np.concatenate([fwd.reshape(P, -1), inv_.reshape(P, -1)], 1).astype(np.float32)
    f = np.float32
    j = np.arange(T, dtype=f)
    bands = (POS_DIM - 1) // 2
    freqs = np.linspace(1e-4, bands - 1, bands, dtype=f)
    a = (f(2.0 * math.pi / T) * j[:, None] * freqs[None, :]).astype(f)
    z = np.concatenate([(j / (T - 1))[:, None], np.cos(a), -np.sin(a)], -1)
    zt = np.zeros((P, T), f)
    zt[:POS_DIM] = z.T
    dist = np.abs(j - T // 2) / (T // 2)
    deltas = np.abs(np.linspace(math.log(1e-2) / 1.5, math.log(1e-2) / 0.3, D, dtype=f))
    window = np.exp(-dist[:, None] * deltas[None, :]).astype(f)
    window = window.reshape(TT, P, D).transpose(1, 0, 2)
    return {"k_small": small, "k_pick": pick.reshape(P, -1), "k_mask": mask.reshape(P, -1), "k_dft": dft,
            "k_pos": zt, "k_window": np.ascontiguousarray(window).reshape(P, -1)}


def build(nc, a, out):
    with ExitStack() as ctx:
        def sb(name, shape, dt=F32):
            return ctx.enter_context(nc.sbuf_tensor(name, shape, dt))

        def sem(name):
            return ctx.enter_context(nc.semaphore(name))

        bank = ctx.enter_context(nc.psum_tensor("bank", [P, 8, NB], F32))
        gu = sb("gu", [P, 4, KT, NB])
        dn = sb("dn", [P, 4, 2, D])
        zone = sb("zone", [P, 10240])
        x = sb("x", [P, TT, D])
        hh = sb("hh", [P, TT, D])
        hc = sb("hc", [P, KT, T])
        hl = sb("hl", [P, KT, T])
        mod = sb("mod", [P, 6, D])
        decay = sb("decay", [P, 2, NB])
        bn = sb("bn", [P, 2, 2, P])
        mr = sb("mr", [P, 2, P])
        cs = sb("cs", [P, KT, 32])
        small = sb("small", [P, C_END])
        par = sb("par", [P, Q_END])
        st = sb("st", [P, 128])

        def const(c, n=P):
            return small[:, c:c + n]

        ident, ones = const(C_IDENT), const(C_ONES)
        cos, sin = const(C_COS, T), const(C_SIN, T)
        off = [0]

        def zv(n, shape, at=None, dt=F32):
            o = off[0] if at is None else at
            off[0] = o + n
            assert off[0] <= 10240
            v = zone[:, o:o + n]
            if dt != F32:
                v = v.bitcast(dt)
            if len(shape) == 1:
                return v
            names = "abcd"[:len(shape)]
            return v.rearrange(f"p ({' '.join(names)}) -> p {' '.join(names)}", **dict(zip(names, shape)))

        def dv(i, shape):
            names = "abcd"[:len(shape)]
            return dn[:, i].rearrange("p f n -> p (f n)").rearrange(
                f"p ({' '.join(names)}) -> p {' '.join(names)}", **dict(zip(names, shape)))

        qz = zv(2048, (2, HEADS, T), at=0)
        cx = zv(2048, (TT, D), at=0)
        qraw = zv(1024, (HEADS, T), at=2048)
        aT = zv(1024, (2, NB), at=2048)
        sgq = zv(1024, (HEADS, T), at=3072)
        amat = zv(1024, (2, NB), at=3072)
        bq = zv(1024, (HEADS, T), at=4096)
        sgk = zv(2048, (HEADS, 2 * T), at=5120)
        modc = zv(2048, (2, D), at=5120)
        cat = zv(2048, (TT, D), at=5120)
        sigbo = zv(1024, (TT, NB), at=7168)
        ex = zv(2048, (2, 2, NB), at=8192)
        wgz = zv(1024, (KT, 2, 64), at=8192)
        wgr = zv(128, (KT, 16), at=9216)
        rope = zv(512, (2, T), at=9344)
        bn_first = zv(512, (2, 2, P), at=9344)
        kk = dv(0, (HEADS, 2 * T))
        av = dv(1, (4, NB))
        bv = dv(2, (4, NB))
        bk = dv(3, (HEADS, 2 * T))
        mask = hh[:, :, :].rearrange("p a (b n) -> p a b n", b=TT)
        pick = mod[:, 0, :].rearrange("p (r m) -> p r m", r=8)
        hgain = mod[:, 1, :].rearrange("p (g n) -> p g n", g=2)
        og = hc[:, :, :].rearrange("p k t -> p (k t)").rearrange("p (g n) -> p g n", g=4)

        ig, fg = ([zone[0:64, 8192 + 512 * j:8704 + 512 * j] for j in range(2)])
        lf, pre = mod[0:64, 1, 0:NB], mod[0:64, 1, NB:D]
        bnf = decay[:, :, :].rearrange("p a n -> p (a n)")
        decay_c, decay_b = bnf[:, 0:2 * T], bnf[:, 2 * T:3 * T]

        ut = zv(6144, (24, T), at=0)
        fw3 = hl[:, :, :].rearrange("p k t -> p (k t)")
        raw3 = decay[:, :, :].rearrange("p a (b t) -> p (a b) t", t=T)
        pos = bn[:, :, :, :].rearrange("p a b n -> p (a b n)")[:, 0:T]
        ys = zv(4096, (4, D), at=6144)
        filt = zv(4096, (TT, 2 * D), at=6144)
        kf = dn[:, :, :, :].rearrange("p r f n -> p r (f n)")
        dfc = hc[:, :, :].rearrange("p k t -> p (k t)")
        dfwd = dfc[:, 0:1024].rearrange("p (t f) -> p t f", t=TT)
        dinv = dfc[:, 1024:2048].rearrange("p (f t) -> p f t", f=4)
        window = mod[:, 3:5, :]
        ztok = hh[:, :, :]

        th = zv(3072, (3, TT, D), at=0, dt=BF16)
        tg = zv(1024, (KT, P))
        ye = zv(1024, (2, NB))
        sg = zv(256, (F,))
        he = zv(256, (F,))
        sg2 = zv(512, (TT, F), at=off[0] - 512)
        hT = zv(256, (2, P))
        pm = zv(256, (T,))
        ptg = zv(256, (TT, P))
        ptb = zv(128, (TT, P), dt=BF16)
        pgc = zv(8, (2, 4))
        rw = zv(512, (KT, E))
        rb = zv(64, (E,))
        sc = zv(128, (TT, E))
        bi = zv(128, (TT, E))
        m8 = zv(128, (TT, NG, 8))
        g12 = zv(24, (TT, 12))
        g12r = zv(24, (TT, 12))
        top = zv(16, (TT, 8))
        gm = zv(16, (TT, NG))
        mk = zv(128, (TT, E))
        pg = zv(4 * (E + OVER + 4), (E + OVER + 4, 4))
        pgo = pg[:, E:E + OVER + 4, :]
        over_at = off[0]
        nx = zv(4, (4,))
        sel = zv(2 * OVER, (2, OVER))
        pgT = zv(512, (4, P))
        over_tiles = zone[:, over_at:off[0]]
        eid = zv(40, (40,), dt=I32)

        mod_row = [nc.dram_tensor(f"mod_row{l}", (1, 6 * D), F32, kind="Internal").ap() for l in range(2)]

        s_const, s_tok, s_lat, s_wg, s_ab = sem("constants_in"), sem("context_in"), sem("latents_in"), sem("gate_w_in"), sem("ab_tables_in")
        chunk_in = [[sem(f"chunk_in{l}{s}") for s in range(4)] for l in range(2)]
        s_bn, s_mr = [sem(f"mod_rows_in{b}") for b in range(2)], [sem(f"mod_stored{b}") for b in range(2)]
        s_silu, s_cbc, s_mod = sem("silu_out"), sem("silu_spread"), sem("mod_spread")
        pick_ps, pick_out = sem("first_rows_ps"), sem("first_rows_out")
        mod_ps, mod_out = sem("mod_ps"), sem("mod_out")
        nrm_ms, nrm_sd, nrm_h = sem("norm_square"), sem("norm_root"), sem("norm_out")
        hT_ps, hT_out = sem("features_ps"), sem("features_out")
        gate_w, gate_ps, gate_x, gate_l = sem("gate_w_rows"), sem("gates_ps"), sem("gates_abs"), sem("gates_log")
        crow = sem("decay_rows")
        bcol_ps, bcol_out = sem("decay_cols_ps"), sem("decay_cols_out")
        proj_ps, proj_out = sem("proj_ps"), sem("proj_out")
        rot_ps, rot_out, s_zero = sem("rot_ps"), sem("rot_out"), sem("query_zero")
        cv_y, cv_s, cv_out = sem("conv_sum"), sem("conv_sigmoid"), sem("conv_out")
        lam_p, lam_ps, lam_e = sem("lambda_products"), sem("lambda_ps"), sem("lambda_exp")
        score_ps, m_ready, e_ready, a_ready = sem("score_ps"), sem("max_out"), sem("exp_out"), sem("weights_out")
        at_ps, at_out, pv_ps, o_out = sem("wT_ps"), sem("wT_out"), sem("value_ps"), sem("heads_out")
        hn_ms, hn_sd, cat_out = sem("head_square"), sem("head_root"), sem("cat_out")
        cT_ps, cT_out = sem("catT_ps"), sem("catT_out")
        mix_ps, mix_sq, mix_ms, mix_sd, x_out = (
            sem("mix_ps"), sem("mix_square"), sem("mix_mean"), sem("mix_root"), sem("x_out"))
        s_hy, s_pos = sem("hy_tables_in"), sem("positions_in")
        f_ps, f_arg, f_sin = sem("filt_ps"), sem("filt_arg"), sem("filt_sin")
        ff_ps, ff_out, kf_ps, kf_out = sem("taps_ps"), sem("taps_out"), sem("spectra_ps"), sem("spectra_out")
        up_ps, up_out = sem("hy_proj_ps"), sem("hy_conv_out")
        vt_ps, vt_out, sp_ps, y_out = sem("hy_T_ps"), sem("hy_T_out"), sem("hy_spec_ps"), sem("hy_prod_out")
        iv_ps, z_out = sem("hy_inv_ps"), sem("hy_gated_out")
        r_in, r_ps, r_sc = sem("router_in"), sem("router_ps"), sem("router_scores")
        r_mk, r_cu, r_pg = sem("router_mask"), sem("router_count_ps"), sem("router_slots")
        r_nx, r_of, r_sel = sem("over_counts"), sem("over_offset_ps"), sem("over_select")
        r_tp, r_to, r_ov, r_id = sem("slotsT_ps"), sem("slotsT_out"), sem("over_ps"), sem("over_ready")
        split_out = sem("split_out")
        sh_ps, sh_sig, sh_h = sem("shared_ps"), sem("shared_sigmoid"), sem("shared_h")
        sh_tp, sh_to, sh_dn = sem("sharedT_ps"), sem("sharedT_out"), sem("shared_down_ps")
        dn_in = sem("shared_down_in")
        over_free = sem("further_done")
        s_out = sem("out_written")
        dve_step = sem("dve_step")
        pool_step = sem("pool_step")

        class Pairs:

            def __init__(self, name, slot_pairs):
                self.gu_in = [sem(f"{name}_gu_in{b}") for b in range(slot_pairs)]
                self.dn_in = [sem(f"{name}_dn_in{b}") for b in range(slot_pairs)]
                self.built, self.step = sem(f"{name}_slots_built"), sem(f"{name}_build_step")
                self.g_ps, self.g_out = sem(f"{name}_gather_ps"), sem(f"{name}_gather_out")
                self.gu_ps, self.sig = sem(f"{name}_gu_ps"), sem(f"{name}_sigmoid")
                self.h, self.hs = sem(f"{name}_h"), sem(f"{name}_h_step")
                self.hT_ps, self.hT_out = sem(f"{name}_hT_ps"), sem(f"{name}_hT_out")
                self.y_ps, self.y_out = sem(f"{name}_y_ps"), sem(f"{name}_y_out")
                self.pT_ps, self.pT_out = sem(f"{name}_pT_ps"), sem(f"{name}_pT_out")

        first = Pairs("first", 2)
        further = [Pairs(f"further{l}", 1) for l in range(2)]

        block = ctx.enter_context(nc.Block())
        N_AB = [4, 4, 2, 4, 4, 4, 4]
        MOD_AB = 18
        CHUNKS = ([("mod", n) for n in range(4)] + [c for n in range(7) for c in (("in", n), ("mod", 4 + 2 * n), ("mod", 5 + 2 * n))]
                  + [("mod", n) for n in range(MOD_AB, 24)] + [("out", 0), ("out", 1), ("sh", 0)],
                  [("in", n) for n in range(6)] + [("out", 0), ("out", 1), ("sh", 0)])
        SHIFT = [2, 2]
        w_mod = [a["w_mod"][l].rearrange("(k p) n -> p k n", p=P) for l in range(2)]
        w_in = [a["w_in_ab"][0].rearrange("(k p) n -> p k n", p=P), a["w_in_hy"][0].rearrange("(k p) n -> p k n", p=P)]
        w_out = [a["w_out_ab"][0].rearrange("(k p) n -> p k n", p=P), a["w_out_hy"][0].rearrange("(k p) n -> p k n", p=P)]

        def slot_of(l, n):
            return (n + SHIFT[l]) % 4

        def chunk_ready(eng, l, n):
            eng.wait_ge(chunk_in[l][slot_of(l, n)], 16 * (n // 4 + 1))

        def chunk_index(l, kind, n):
            return CHUNKS[l].index((kind, n))

        def unit_read(u):
            if u < 4:
                return proj_out, u + 1
            if u < 8:
                return cv_y, u - 3
            if u < 18:
                return proj_out, u - 3
            if u < 22:
                return cv_y, u - 13
            return proj_out, u - 7

        def mod_rows(n):
            return (bn_first if n in (2, 3) else bn)[:, n % 2]

        def rows_in(n):
            return 16 * max(n // 2 + 1, 2)

        def mod_bank(n):
            return 6 + n % 2 if n < MOD_AB else 2 + 3 * (n % 2)

        def turn_bank(i, n, t):
            return t if i and not n else 4 + t + 2 * n * (1 - i)

        def norm_col(i, t):
            return 96 + 4 * t if i != 1 else (120, 92)[t]

        def stored(n):
            return 16 * (n // 2 - 1)

        def chunk_used(l, n):
            kind, c = CHUNKS[l][n]
            if kind == "mod":
                return mod_ps, c + 1
            if kind == "in":
                return (proj_ps, sum(N_AB[:c + 1])) if l == 0 else (up_ps, 4 * (c + 1))
            if kind == "out":
                return mix_ps, 4 * l + 2 * (c + 1)
            return sh_ps, 2 * (l + 1)

        @block.sync
        def _(sp):
            sp.dma_start(small[:, :], a["k_small"]).then_inc(s_const, 16)
            sp.dma_start(par[:, :], a["params"]).then_inc(s_const, 16)

            def chunks(l):
                for n, (kind, c) in enumerate(CHUNKS[l]):
                    if l == 0 and n == 4:
                        sp.dma_start(cx[:, :, :], a["ctx"][0].rearrange("(t p) d -> p t d", p=P)).then_inc(s_tok, 16)
                        sp.dma_start(x[:, :, :], a["x"][0].rearrange("(t p) d -> p t d", p=P)).then_inc(s_lat, 16)
                    if n >= 4:
                        sp.wait_ge(*chunk_used(l, n - 4))
                    elif l == 1 and n < 2:
                        sp.wait_ge(first.gu_ps, PAIRS)
                    elif l == 1 and n == 2:
                        sp.wait_ge(over_free, 1)
                    cols = slice(c % 12 * NB, (c % 12 + 1) * NB)
                    src = {"mod": w_mod[c // 12], "in": w_in[l], "out": w_out[l]}
                    src = a["sh_gu"][l].rearrange("(k p) n -> p k n", p=P) if kind == "sh" else src[kind][:, :, cols]
                    s = slot_of(l, n)
                    sp.dma_start(gu[:, s], src).then_inc(chunk_in[l][s], 16)
                if l == 0:
                    sp.wait_ge(pv_ps, 16)
                else:
                    sp.wait_ge(y_out, 4)
                sp.dma_start(dn[:, 3], a["sh_down"][l].rearrange("(f p) n -> p f n", p=P)).then_inc(dn_in, 16)

            def expert(l, e, j, ph):
                sp.dma_start(gu[:, j], a["exp_gu"][l][bass.ds(e, 1)].rearrange("a (k p) n -> p (a k) n", p=P)).then_inc(
                    ph.gu_in[j // 2], 16)

            def expert_down(l, e, j, ph):
                sp.dma_start(dn[:, j], a["exp_down"][l][bass.ds(e, 1)].rearrange("a (f p) n -> p (a f) n", p=P)).then_inc(
                    ph.dn_in[j // 2], 16)

            for l in range(2):
                chunks(l)
                last = len(CHUNKS[l])
                for b in range(2):
                    for j in range(2):
                        s = 2 * b + j
                        n = max(m for m in range(last) if slot_of(l, m) == s)
                        sp.wait_ge(*chunk_used(l, n))
                        expert(l, s, s, first)
                    for j in range(2 - b):
                        expert_down(l, 2 * b + j, 2 * b + j, first)

                def next_up(i, b):
                    sp.wait_ge(first.gu_ps, 2 * i + (b - 1 + PAIRS * l))
                    expert(l, 4 * i + 2 * b, 2 * b, first)
                    expert(l, 4 * i + (2 * b + 1), 2 * b + 1, first)

                def next_down(i, b):
                    sp.wait_ge(first.y_ps, 4 * i + 2 * (b - 1 + PAIRS * l))
                    expert_down(l, 4 * i + 2 * b, 2 * b, first)
                    expert_down(l, 4 * i + (2 * b + 1), 2 * b + 1, first)

                next_up(1, 0)
                sp.wait_ge(sh_dn, l + 1)
                expert_down(l, 3, 3, first)
                next_down(1, 0)
                sp.wait_ge(r_id, l + 1)
                n = sp.value_load(eid[0:1, 36:37], min_val=1, max_val=OVER // 2)
                next_up(1, 1)
                next_down(1, 1)
                with sp.Fori(2, PAIRS // 2) as i:
                    for b in range(2):
                        next_up(i, b)
                        next_down(i, b)
                ph = further[l]
                sp.wait_ge(first.gu_ps, PAIRS * (l + 1) - 1)
                sp.wait_ge(first.y_ps, 2 * (PAIRS * (l + 1) - 1))
                with sp.Fori(0, n) as i:
                    sp.wait_ge(ph.gu_ps, i + 1)
                    es = [sp.value_load(eid[0:1, bass.ds(2 * i + j, 1)], min_val=0, max_val=E - 1) for j in range(2)]
                    for j in range(2):
                        expert(l, es[j], j, ph)
                    sp.wait_ge(ph.y_ps, 2 * i + 2)
                    for j in range(2):
                        expert_down(l, es[j], j, ph)
            for t in range(TT):
                sp.wait_ge(x_out, 7 + t)
                sp.dma_start(out[0, t * P:(t + 1) * P, :], x[:, t, :]).then_inc(s_out, 16)
            sp.wait_ge(s_out, 32)

        @block.gpsimd
        def _(pool):
            steps = [0]

            def step(ins):
                steps[0] += 1
                ins.then_inc(pool_step, 1)
                pool.wait_ge(pool_step, steps[0])

            def mod_load(n):
                pool.dma_start(mod_rows(n), a["mod_rows"][n]).then_inc(s_bn[n % 2], 16)

            def mod_store(n):
                pool.wait_ge(mod_out, n + 1)
                pool.dma_start(mod_row[n // 12][0, n % 12 * NB:(n % 12 + 1) * NB].rearrange("(j n) -> j n", j=4),
                               mr[0:P:32, n % 2, :]).then_inc(s_mr[n % 2], 16)

            def mod_spread(l, lo, hi):
                for b in range(2):
                    pool.wait_ge(s_mr[b], stored(12 * l + 2 * hi - 2 + b))
                pool.dma_start(mod[:, lo:hi, :].rearrange("p m n -> p (m n)"),
                               mod_row[l][0:1, lo * D:hi * D].broadcast_to([P, (hi - lo) * D])).then_inc(s_mod, 16)

            def router_loads(l):
                pool.wait_ge(x_out, 4 * l + 2)
                pool.dma_start(rw, a["router_w"][l].rearrange("(k p) e -> p k e", p=P)).then_inc(r_in, 16)
                pool.dma_start(rb, a["router_b"][l:l + 1].broadcast_to([P, E])).then_inc(r_in, 16)

            def moe(l):
                pool.wait_ge(nrm_h, 2 * (2 if l == 0 else 4) + 1)
                pool.wait_ge(hT_ps, 2 * (2 * (2 if l == 0 else 4) + 1))
                for q in range(2):
                    step(nc.gpsimd.tensor_copy(th[:, q, 0, :], hh[:, 0, :]))
                    step(nc.gpsimd.tensor_tensor(hh[:, 0, :], hh[:, 0, :], th[:, q, 0, :], ALU.subtract))
                nc.gpsimd.tensor_copy(th[:, 2, 0, :], hh[:, 0, :]).then_inc(split_out, 1)

            for n in range(4):
                mod_load(n)
            for n in range(2):
                pool.wait_ge(mod_out, n + 1)
                mod_load(n + 4)
            pool.wait_ge(nrm_h, 4)
            pool.dma_start(mod[:, 0, :], a["k_pick"]).then_inc(s_ab, 16)
            nc.gpsimd.memset(qz[:, :, :, :].rearrange("p a b c -> p (a b c)"), 0.0).then_inc(s_zero, 1)
            pool.wait_ge(hT_ps, 8)
            pool.dma_start(mask, a["k_mask"].rearrange("p (a b n) -> p a b n", a=2, b=TT)).then_inc(s_ab, 16)
            pool.wait_ge(crow, 1)
            for g, name in enumerate(("head_g_a", "head_g_b")):
                pool.dma_start(hgain[:, g, :], a[name][0:1].broadcast_to([P, NB])).then_inc(s_ab, 16)
            for n in range(4, 24):
                mod_store(n)
                if n + 2 < 24:
                    mod_load(n + 2)
                if n == 11:
                    mod_spread(0, 2, 6)
            router_loads(0)
            pool.wait_ge(x_out, 2)
            mod_spread(1, 0, 3)
            moe(0)
            pool.wait_ge(nrm_h, 6)
            pool.dma_start(window, a["k_window"].rearrange("p (t n) -> p t n", t=TT)).then_inc(s_hy, 16)
            pool.dma_start(dfc, a["k_dft"]).then_inc(s_hy, 16)
            pool.dma_start(pos, a["k_pos"]).then_inc(s_pos, 16)
            pool.wait_ge(r_ps, 1)
            pool.wait_ge(sh_ps, 2)
            pool.dma_start(fw3, a["filt_w3"]).then_inc(s_hy, 16)
            pool.wait_ge(ff_out, 8)
            pool.wait_ge(x_out, 4)
            mod_spread(1, 3, 6)
            router_loads(1)
            moe(1)

        @block.tensor
        def _(pe):
            def mm(o, lhsT, rhs, start, stop):
                return pe.matmul(o, lhsT, rhs, start=start, stop=stop, skip_group_check=True)

            def mod_chunk(n):
                i = chunk_index(0, "mod", n)
                chunk_ready(pe, 0, i)
                if n >= 2:
                    pe.wait_ge(mod_out, n - 1)
                w = gu[:, slot_of(0, i)]
                for k in range(KT):
                    for j in range(4):
                        last = mm(bank[32 * j:32 * (j + 1), mod_bank(n), 0:P], cs[:, k, :], w[:, k, j * P:(j + 1) * P], k == 0, k == KT - 1)
                last.then_inc(mod_ps, 1)

            def first_rows(n):
                pe.wait_ge(mod_out, n + 1)
                if n >= 2:
                    pe.wait_ge(pick_out, 2 * (n - 1))
                for r in (1, 0):
                    for j in range(4):
                        row = ident[:, 32 * j + 16 * r:32 * j + 16 * r + 1].broadcast_to([P, P])
                        last = mm(bank[:, 2 * (n % 2) + r, j * P:(j + 1) * P], row, mr[:, n % 2, :], True, True)
                    last.then_inc(pick_ps, 1)

            def features(i, t):
                pe.wait_ge(nrm_h, 2 * i + t + 1)
                for g in range(2):
                    q = 2 * (2 * i + t) + g
                    if q >= 2:
                        pe.wait_ge(hT_out, q - 1)
                    for k in range(4):
                        last = pe.transpose(bank[:, 6 + g, k * P:(k + 1) * P], hh[:, t, (4 * g + k) * P:(4 * g + k + 1) * P], ident)
                    last.then_inc(hT_ps, 1)

            def gates(half):
                pe.wait_ge(hT_out, 4 * half + 4)
                pe.wait_ge(gate_w, 1)
                for k in range(KT):
                    last = mm(bank[:, 4, half * T:(half + 1) * T], wgz[:, k, :, :].rearrange("p f m -> p (f m)"), (hc, hl)[half][:, k, :],
                              k == 0, k == KT - 1)
                last.then_inc(gate_ps, 1)

            def project_ab():
                u = 0
                for c, n_units in enumerate(N_AB):
                    n = chunk_index(0, "in", c)
                    chunk_ready(pe, 0, n)
                    w = gu[:, slot_of(0, n)]
                    for j in range(n_units):
                        if u >= 4:
                            pe.wait_ge(*unit_read(u - 4))
                        o = bank[:, u % 4, :]
                        if c in (0, 1):
                            for k in range(KT):
                                last = mm(o[:, 0:T], w[:, k, j * P:(j + 1) * P], hl[:, k, :], k == 0, k == KT - 1)
                        elif c in (3, 5):
                            for half, tok in enumerate((hc, hl)):
                                for k in range(KT):
                                    last = mm(o[:, half * T:(half + 1) * T], w[:, k, j * P:(j + 1) * P], tok[:, k, :], k == 0, k == KT - 1)
                        else:
                            tok = hl if c == 2 or j >= 2 else hc
                            for k in range(KT):
                                last = mm(o, tok[:, k, (j % 2) * P:(j % 2 + 1) * P], w[:, k, :], k == 0, k == KT - 1)
                        last.then_inc(proj_ps, 1)
                        u += 1
                    if c == 3:
                        lambda_and_decay()
                    elif c in (4, 5):
                        ropes(2 * c - 8)
                    for n in range(4 + 2 * c, 6 + 2 * c):
                        mod_chunk(n)

            def ropes(first_q):
                pe.wait_ge(*unit_read(13))
                for q in range(first_q, first_q + 2):
                    if q == 0:
                        pe.wait_ge(lam_e, 1)
                        pe.wait_ge(bcol_out, 1)
                    elif q >= 2:
                        pe.wait_ge(rot_out, q - 1)
                    for j in range(2):
                        h = 2 * (q % 2) + j
                        src = qraw[:, h, :] if q < 2 else kk[:, h, T:2 * T]
                        last = mm(bank[:, 4 + q % 2, j * T:(j + 1) * T], const(C_ROT), src, True, True)
                    last.then_inc(rot_ps, 1)

            def lambda_and_decay():
                pe.wait_ge(lam_p, 1)
                pe.wait_ge(gate_x, 1)
                mm(bank[:, 4, 0:2], ones, st[:, 0:2], True, True).then_inc(lam_ps, 1)
                pe.wait_ge(crow, 1)
                mm(bank[:, 5, 0:8], ones, st[:, 8:16], True, True)
                for t in range(TT):
                    last = pe.transpose(bank[:, 5, (1 + t) * P:(2 + t) * P], decay_b[:, t * P:(t + 1) * P], ident)
                last.then_inc(bcol_ps, 1)

            def scores(u):
                g, h, b = u // 4, u % 4, 3 * (u % 2)
                t = g % 2
                if u == 0:
                    pe.wait_ge(rot_out, 4)
                    pe.wait_ge(*unit_read(21))
                    pe.wait_ge(*unit_read(25))
                if u == 8:
                    pe.wait_ge(cv_out, 8)
                    pe.wait_ge(mod_out, 24)
                    pe.wait_ge(s_ab, 64)
                if u >= 2:
                    pe.wait_ge(a_ready, u - 1)
                tok = slice(t * P, (t + 1) * P)
                if g < 2:
                    for c in range(2):
                        last = mm(bank[:, b + c, :], qz[:, c, h, tok], kk[:, h, :], True, True)
                else:
                    mm(bank[:, b, :], bq[:, h, tok], bk[:, h, :], True, True)
                    for d in range(2):
                        last = mm(bank[:, b + 1 + d, :], pick[:, 4 * d + h, :], decay_c, True, True)
                last.then_inc(score_ps, 1)

            def values(u):
                g, h = u // 4, u % 4
                pe.wait_ge(a_ready, u + 1)
                if u:
                    pe.wait_ge(at_out, u)
                for j in range(4):
                    last = pe.transpose(bank[:, 6, j * P:(j + 1) * P], amat[:, u % 2, j * P:(j + 1) * P], ident)
                last.then_inc(at_ps, 1)
                pe.wait_ge(at_out, u + 1)
                if h == 0 and g:
                    pe.wait_ge(o_out, g)
                v = av if g < 2 else bv
                for j in range(4):
                    last = mm(bank[:, 7, h * DV:(h + 1) * DV], aT[:, u % 2, j * P:(j + 1) * P], v[:, j, h * DV:(h + 1) * DV],
                              j == 0, j == 3)
                last.then_inc(pv_ps, 1)

            def out_ab():
                pe.wait_ge(at_out, 16)
                pe.wait_ge(o_out, 4)
                for t in range(TT):
                    pe.wait_ge(cat_out, 2 * t + 2)
                    for g in range(2):
                        if t:
                            pe.wait_ge(cT_out, g + 1)
                        for k in range(4):
                            last = pe.transpose(bank[:, 6 + g, k * P:(k + 1) * P], cat[:, t, (4 * g + k) * P:(4 * g + k + 1) * P], ident)
                        last.then_inc(cT_ps, 1)
                pe.wait_ge(cT_out, 4)
                mix_out(0, hl)

            def mix_out(l, src):
                for n in range(HALVES):
                    i = chunk_index(l, "out", n)
                    chunk_ready(pe, l, i)
                    for t in range(TT):
                        for k in range(KT):
                            last = mm(bank[:, 2 * t + n, :], src[:, k, t * P:(t + 1) * P], gu[:, slot_of(l, i), k, :], k == 0, k == KT - 1)
                        last.then_inc(mix_ps, 1)

            def filter_layer(i):
                if i == 0:
                    pe.wait_ge(s_pos, 16)
                else:
                    pe.wait_ge(f_sin, 1)
                mm(bank[0:HIDDEN, 6, 0:T], par[:, (Q_W1, Q_W2)[i]:(Q_W1, Q_W2)[i] + HIDDEN], raw3[:, 0, :] if i else pos,
                   True, True).then_inc(f_ps, 1)

            def filter_taps():
                pe.wait_ge(f_sin, 2)
                pe.wait_ge(s_hy, 48)
                for u in range(8):
                    t, n = u // 4, u % 4
                    if u >= 2:
                        pe.wait_ge(ff_out, u - 1)
                    mm(bank[:, 5 + u % 2, :], raw3[:, 0, t * P:(t + 1) * P], fw3[:, n * NB:(n + 1) * NB], True, True).then_inc(ff_ps, 1)
                pe.wait_ge(ff_out, 8)
                pe.wait_ge(mix_sq, 8)
                for u in range(16):
                    f, n = u % 4, u // 4
                    if u >= 2:
                        pe.wait_ge(kf_out, u - 1)
                    for t in range(TT):
                        last = mm(bank[:, 4 + u % 2, :], dfwd[:, t, f * P:(f + 1) * P], filt[:, t, n * NB:(n + 1) * NB], t == 0, t == 1)
                    last.then_inc(kf_ps, 1)

            def hyena():
                pe.wait_ge(hT_out, 16)
                for u in range(24):
                    c, j = u // 4, u % 4
                    if j == 0:
                        chunk_ready(pe, 1, c)
                    if u >= 4:
                        pe.wait_ge(up_out, u - 3)
                    for k in range(KT):
                        last = mm(bank[:, u % 4, 0:T], gu[:, slot_of(1, c), k, j * P:(j + 1) * P], hl[:, k, :], k == 0, k == KT - 1)
                    last.then_inc(up_ps, 1)
                for i in range(2):
                    for n in range(HALVES):
                        if i == 0:
                            pe.wait_ge(up_out, 8)
                            pe.wait_ge(kf_out, 16)
                        else:
                            pe.wait_ge(z_out, 4 * (n + 1))
                        for t in range(TT):
                            for k in range(4):
                                last = pe.transpose(bank[:, turn_bank(i, n, t), k * P:(k + 1) * P], ut[:, 4 * n + k, t * P:(t + 1) * P], ident)
                            last.then_inc(vt_ps, 1)
                        if i == 0 and n == 0:
                            pe.wait_ge(up_out, 24)
                        pe.wait_ge(vt_out, 4 * i + 2 * n + 2)
                        for f in range(4):
                            for t in range(TT):
                                last = mm(bank[:, 4 * n + f, :], dfwd[:, t, f * P:(f + 1) * P], ztok[:, t, n * NB:(n + 1) * NB], t == 0, t == 1)
                        last.then_inc(sp_ps, 1)
                    for c in range(8):
                        if c % 4 == 0:
                            pe.wait_ge(y_out, 2 * i + c // 4 + 1)
                        for f in range(4):
                            last = mm(bank[:, c, 0:T], ys[:, f, c * P:(c + 1) * P], dinv[:, f, :], f == 0, f == 3)
                        last.then_inc(iv_ps, 1)
                pe.wait_ge(z_out, 16)
                mix_out(1, ut)

            def shared_expert(l, t):
                i = chunk_index(l, "sh", 0)
                w = gu[:, slot_of(l, i)]
                chunk_ready(pe, l, i)
                pe.wait_ge(hT_out, 4 * (2 if l == 0 else 4) + 2 * (t + 1))
                for k in range(KT):
                    last = mm(bank[:, 4 + t, :], hl[:, k, t * P:(t + 1) * P], w[:, k, :], k == 0, k == KT - 1)
                last.then_inc(sh_ps, 1)

            def shared_down(l):
                pe.wait_ge(dn_in, 16 * (l + 1))
                pe.wait_ge(first.pT_out, (PAIRS + 1) * l + 1)
                pe.wait_ge(x_out, 4 * l + 2)
                for t in range(TT):
                    pe.wait_ge(sh_h, 2 * l + t + 1)
                    for f in range(2):
                        last = pe.transpose(bank[:, 7, f * P:(f + 1) * P], sg2[:, t, f * P:(f + 1) * P], ident)
                    last.then_inc(sh_tp, 1)
                    pe.wait_ge(sh_to, 2 * l + t + 1)
                    for n in range(HALVES):
                        for f in range(2):
                            last = mm(bank[:, 2 * t + n, :], hT[:, f, :], dn[:, 3, f, n * NB:(n + 1) * NB], f == 0, False)
                last.then_inc(sh_dn, 1)

            def route(l):
                pe.wait_ge(r_in, 32 * (l + 1))
                pe.wait_ge(hT_out, 4 * (2 if l == 0 else 4) + 4)
                for t in range(TT):
                    for k in range(KT):
                        last = mm(bank[:, 6, t * E:(t + 1) * E], hl[:, k, t * P:(t + 1) * P], rw[:, k, :], k == 0, k == KT - 1)
                last.then_inc(r_ps, 1)

            def route_slots(l):
                pe.wait_ge(r_mk, l + 1)
                mm(bank[:, 6, 128:192], const(C_TRI), mk[:, 0, :], True, True)
                mm(bank[:, 6, 192:256], ones, mk[:, 0, :], True, False)
                mm(bank[:, 6, 192:256], const(C_TRI), mk[:, 1, :], False, True)
                mm(bank[0:E, 6, 256:257], mk[:, 0, :], const(C_ONES, 1), True, False)
                mm(bank[0:E, 6, 256:257], mk[:, 1, :], const(C_ONES, 1), False, True).then_inc(r_cu, 1)

            def route_over(l):
                pe.wait_ge(r_nx, l + 1)
                mm(bank[0:E, 6, 258:259], const(C_TRI, E), nx[:, 0:1], True, True)
                mm(bank[:, 6, 260:261], ones, nx[:, 0:1], True, True).then_inc(r_of, 1)

            def route_list(l):
                pe.wait_ge(r_sel, l + 1)
                for j in range(4):
                    last = pe.transpose(bank[0:E, 7, j * P:(j + 1) * P], pg[:, 0:E, j], ident)
                last.then_inc(r_tp, 1)
                pe.wait_ge(r_to, l + 1)
                for j in range(4):
                    o = bank[:, 6, j * OVER:(j + 1) * OVER]
                    mm(o, pgT[:, j, :], sel[:, 0, :], True, j >= 2)
                    if j < 2:
                        mm(o, ones, sel[:, 1, :], False, True)
                mm(bank[0:1, 6, 4 * OVER:5 * OVER], const(C_E, 1), sel[:, 0, :], True, True).then_inc(r_ov, 1)

            def gather(p, ph, gb, half):
                for k in range(4 * half, 4 * half + 4):
                    o = bank[:, 4 + 2 * half, (k % 4) * P:(k % 4 + 1) * P]
                    for t in range(TT):
                        for q in range(3):
                            last = mm(o, th[:, q, t, k * P:(k + 1) * P], ptb[:, t, :], t == 0 and q == 0, t == 1 and q == 2)
                last.then_inc(ph.g_ps, 1)

            def slots_t(ph):
                for t in range(TT):
                    last = pe.transpose(bank[:, 7, t * P:(t + 1) * P], ptg[:, t, :], ident)
                last.then_inc(ph.pT_ps, 1)

            def prologue(ph, gb):
                pe.wait_ge(ph.built, gb + 1)
                gather(0, ph, gb, 0)
                gather(0, ph, gb, 1)
                slots_t(ph)

            def pair_up(p, ph, gb, slots, uses):
                pe.wait_ge(ph.gu_in[slots[0] // 2], uses)
                pe.wait_ge(ph.g_out, 2 * p + (2 * gb + 2))
                for k in range(KT):
                    for j, s in enumerate(slots):
                        last = mm(bank[C * j:C * (j + 1), 5, :], tg[:, k, C * j:C * (j + 1)], gu[:, s, k, :], k == 0, k == KT - 1)
                last.then_inc(ph.gu_ps, 1)

            def pair_down(p, ph, gb, nb, slots, uses):
                pe.wait_ge(ph.built, p + (gb + 2))
                gather(p, ph, gb, 0)
                pe.wait_ge(ph.h, p + (nb + 1))
                pe.wait_ge(ph.pT_out, p + (gb + 1))
                for f in range(2):
                    last = pe.transpose(bank[:, 7, f * P:(f + 1) * P], he[:, f * P:(f + 1) * P], ident)
                last.then_inc(ph.hT_ps, 1)
                gather(p, ph, gb, 1)
                pe.wait_ge(ph.hT_out, p + (nb + 1))
                pe.wait_ge(ph.dn_in[slots[0] // 2], uses)
                for n, o in enumerate((5, 6)):
                    if n:
                        pe.wait_ge(ph.g_out, 2 * p + (2 * gb + 4))
                    for f in range(2):
                        for j, s in enumerate(slots):
                            last = mm(bank[C * j:C * (j + 1), o, :], hT[:, f, C * j:C * (j + 1)], dn[:, s, f, n * NB:(n + 1) * NB], f == 0, f == 1)
                    last.then_inc(ph.y_ps, 1)
                for n in range(HALVES):
                    pe.wait_ge(ph.y_out, 2 * p + (2 * nb + n + 1))
                    for t in range(TT):
                        last = mm(bank[:, 2 * t + n, :], pm[:, t * P:(t + 1) * P], ye[:, n, :], False, False)
                slots_t(ph)

            def pair(p, ph, gb, nb, slots, uses):
                pair_up(p, ph, gb, slots, uses)
                pair_down(p, ph, gb, nb, slots, uses)

            def moe(l):
                gb, nb = (PAIRS + 1) * l, PAIRS * l
                features(2 * l + 2, 0)
                shared_expert(l, 0)
                features(2 * l + 2, 1)
                route(l)
                shared_expert(l, 1)
                route_slots(l)
                pe.wait_ge(split_out, 2 * (l + 1))
                pe.wait_ge(sh_h, 2 * l + 2)
                ph = further[l]
                pe.nop("credit").then_inc(ph.gu_ps, 1)
                pe.nop("credit").then_inc(ph.y_ps, 2)
                prologue(first, gb)
                uses = 16 * PAIRS * l + 32
                pair_up(0, first, gb, (0, 1), uses)
                route_over(l)
                shared_down(l)
                route_list(l)
                pe.wait_ge(r_id, l + 1)
                n = pe.value_load(eid[0:1, 36:37], min_val=1, max_val=OVER // 2)
                pair_down(0, first, gb, nb, (0, 1), uses)
                if l == 0:
                    filter_layer(0)
                pair_up(1, first, gb, (2, 3), uses)
                if l == 0:
                    pe.wait_ge(f_arg, 1)
                pair_down(1, first, gb, nb, (2, 3), uses)
                if l == 0:
                    filter_layer(1)
                with pe.Fori(1, PAIRS // 2) as i:
                    for b in range(2):
                        uses = 32 * i + 32 * (l * (PAIRS // 2) + 1)
                        pair_up(2 * i + b, first, gb, (2 * b, 2 * b + 1), uses)
                        if b == 0:
                            pe.wait_ge(f_arg, 2)
                        pair_down(2 * i + b, first, gb, nb, (2 * b, 2 * b + 1), uses)
                pe.wait_ge(first.g_out, 2 * (gb + PAIRS + 1))
                pe.wait_ge(first.pT_out, gb + PAIRS + 1)
                for sem_, value in ((ph.step, 1), (ph.built, 1), (ph.g_ps, 2), (ph.g_out, 2), (ph.pT_ps, 1), (ph.pT_out, 1)):
                    pe.nop("credit").then_inc(sem_, value)
                with pe.Fori(0, n) as i:
                    pair(i, ph, 0, 0, (0, 1), 32 * i + 32)
                for b in range(4):
                    last = mm(bank[:, b, 0:1], ident, st[:, 127:128], False, True)
                last.then_inc(over_free, 1)

            pe.wait_ge(s_const, 32)
            pe.wait_ge(s_cbc, 2)
            mod_chunk(0)
            for n in range(1, 4):
                mod_chunk(n)
                first_rows(n - 1)
            first_rows(3)
            for i in range(2):
                for t in range(TT):
                    features(i, t)
                gates(i)
            project_ab()
            scores(0)
            for u in range(16):
                if u < 15:
                    scores(u + 1)
                values(u)
                if u < 24 - MOD_AB:
                    mod_chunk(MOD_AB + u)
            out_ab()
            moe(0)
            filter_taps()
            for t in range(TT):
                features(3, t)
            hyena()
            moe(1)

        @block.scalar
        def _(act):
            def act_fn(o, i, f, **kw):
                return nc.scalar.activation(o, i, f, **kw)

            def root(i, t):
                act.wait_ge(nrm_ms, 2 * i + t + 1)
                s = norm_col(i, t)
                act_fn(st[:, s + 2:s + 3], st[:, s + 1:s + 2], ACT.Sqrt).then_inc(nrm_sd, 1)

            def features(i, t):
                dst = hc if i == 0 else hl
                for g in range(2):
                    act.wait_ge(hT_ps, 2 * (2 * i + t) + g + 1)
                    act_fn(dst[:, 4 * g:4 * g + 4, t * P:(t + 1) * P], bank[:, 6 + g, :].rearrange("p (k n) -> p k n", k=4),
                           ACT.Copy).then_inc(hT_out, 1)

            def units(lo, hi):
                for u in range(lo, hi):
                    act.wait_ge(proj_ps, u + 1)
                    if u == 10:
                        act.wait_ge(hT_ps, 8)
                    src = bank[:, u % 4, :]
                    if u < 4:
                        ins = act_fn(qraw[:, u, :], src[:, 0:T], ACT.Copy)
                    elif u < 10:
                        ins = act_fn(sigbo[:, u - 8, :], src, ACT.Sigmoid)
                    elif u < 14:
                        ins = act_fn(kk[:, u - 10, :], src, ACT.Copy)
                    elif u < 18:
                        ins = act_fn(av[:, u - 14, :], src, ACT.Copy)
                    else:
                        ins = act_fn(bv[:, u - 22, :], src, ACT.Copy)
                    ins.then_inc(proj_out, 1)

            def exps(u):
                g, s, b = u // 4, 40 + 16 * (u % 2), 3 * (u % 2)
                act.wait_ge(m_ready, u + 1)
                if g < 2:
                    for c in range(2):
                        act_fn(ex[:, u % 2, c, :], bank[:, b + c, :], ACT.Exp, bias=st[:, s + 2 + c:s + 3 + c], scale=DQK ** -0.5,
                               accum_out=st[:, s + 6 + c:s + 7 + c]).then_inc(e_ready, 1)
                else:
                    for d in range(2):
                        act_fn(ex[:, u % 2, d, :], ex[:, u % 2, d, :], ACT.Exp, bias=st[:, s + 2 + d:s + 3 + d]).then_inc(e_ready, 1)
                    act_fn(st[:, s + 8:s + 10], st[:, s + 4:s + 6], ACT.Exp).then_inc(e_ready, 1)

            def post_squares(t):
                for n in range(HALVES):
                    act_fn(hh[:, t, n * NB:(n + 1) * NB], bank[:, 2 * t + n, :], ACT.Square,
                           accum_out=st[:, 80 + 2 * t + n:81 + 2 * t + n]).then_inc(mix_sq, 1)

            def post_root(j, t):
                act.wait_ge(mix_ms, 2 * j + t + 1)
                act_fn(st[:, 88 + t:89 + t], st[:, 86 + t:87 + t], ACT.Sqrt).then_inc(mix_sd, 1)

            def after_mixer(l):
                i = 2 * l + 2
                act.wait_ge(mix_ps, 4 * l + 3)
                post_squares(0)
                post_root(2 * l, 0)
                root(i, 0)
                act.wait_ge(mix_ps, 4 * l + 4)
                post_squares(1)
                features(i, 0)
                post_root(2 * l, 1)
                root(i, 1)
                features(i, 1)

            def first_pass(ph, p, gb, nb, c):
                act.wait_ge(ph.gu_ps, p + (nb + 1 + c))
                act_fn(sg, bank[:, 5, 0:F], ACT.Sigmoid).then_inc(ph.sig, 1)
                gathered(ph, 2 * p + (2 * gb + 3), 0)
                act.wait_ge(ph.hT_ps, p + (nb + 1))
                act_fn(hT[:, :, :].rearrange("p f n -> p (f n)"), bank[:, 7, 0:F], ACT.Copy).then_inc(ph.hT_out, 1)
                gathered(ph, 2 * p + (2 * gb + 4), 1)
                slots(ph, p + (gb + 2))

            def gathered(ph, value, half):
                act.wait_ge(ph.g_ps, value)
                act_fn(tg[:, 4 * half:4 * half + 4, :].rearrange("p k n -> p (k n)"), bank[:, 4 + 2 * half, :], ACT.Copy).then_inc(ph.g_out, 1)

            def slots(ph, value):
                act.wait_ge(ph.pT_ps, value)
                act_fn(pm, bank[:, 7, 0:T], ACT.Copy).then_inc(ph.pT_out, 1)

            def sine(i):
                act.wait_ge(f_arg, i + 1)
                act_fn(raw3[0:HIDDEN, 0, :], raw3[0:HIDDEN, 1, :], ACT.Sin).then_inc(f_sin, 1)

            def moe(l):
                gb, nb = (PAIRS + 1) * l, PAIRS * l
                act.wait_ge(r_ps, l + 1)
                act_fn(sc[:, :, :].rearrange("p t e -> p (t e)"), bank[:, 6, 0:TT * E], ACT.Sigmoid).then_inc(r_sc, 1)
                for t in range(TT):
                    act.wait_ge(sh_ps, 2 * l + t + 1)
                    act_fn(sg2[:, t, :], bank[:, 4 + t, 0:F], ACT.Sigmoid).then_inc(sh_sig, 1)
                for half in range(2):
                    gathered(first, 2 * gb + half + 1, half)
                slots(first, gb + 1)
                for t in range(TT):
                    act.wait_ge(sh_tp, 2 * l + t + 1)
                    act_fn(hT[:, :, :].rearrange("p f n -> p (f n)"), bank[:, 7, 0:F], ACT.Copy).then_inc(sh_to, 1)
                act.wait_ge(r_tp, l + 1)
                act_fn(pgT[0:E, :, :].rearrange("p j n -> p (j n)"), bank[0:E, 7, :], ACT.Copy).then_inc(r_to, 1)
                act.wait_ge(r_id, l + 1)
                n = act.value_load(eid[0:1, 36:37], min_val=1, max_val=OVER // 2)
                for p in range(2):
                    first_pass(first, p, gb, nb, 0)
                    if l == 0:
                        sine(p)
                with act.Fori(1, PAIRS // 2) as i:
                    for b in range(2):
                        first_pass(first, 2 * i + b, gb, nb, 0)
                ph = further[l]
                with act.Fori(0, n) as i:
                    first_pass(ph, i, 0, 0, 1)
                act.wait_ge(over_free, l + 1)
                for t in range(TT):
                    post_squares(t)
                for t in range(TT):
                    post_root(2 * l + 1, t)

            act.dma_start(wgr, w_in[0][:, :, 7 * NB:7 * NB + 16]).then_inc(s_wg, 16)
            act.wait_ge(s_const, 32)
            act.wait_ge(dve_step, 1)
            act_fn(st[:, 64:80], par[:, Q_C:Q_C + 16], ACT.Sigmoid).then_inc(s_silu, 1)
            for n in range(4):
                for r, o in enumerate((modc, mod)):
                    act.wait_ge(pick_ps, 2 * n + r + 1)
                    act_fn(o[:, n // 2, n % 2 * NB:(n % 2 + 1) * NB], bank[:, 2 * (n % 2) + 1 - r, :], ACT.Copy).then_inc(pick_out, 1)
            for i in range(2):
                for t in range(TT):
                    root(i, t)
                for t in range(TT):
                    features(i, t)
            act.wait_ge(gate_x, 1)
            act_fn(lf, lf, ACT.Exp).then_inc(gate_l, 1)
            act.wait_ge(gate_l, 1)
            act_fn(lf, lf, ACT.Ln, bias=1.0).then_inc(gate_l, 1)
            units(0, 4)
            for u in range(HEADS):
                act.wait_ge(cv_y, u + 1)
                act_fn(sgq[:, u, :], bq[:, u, :], ACT.Sigmoid).then_inc(cv_s, 1)
            units(8, 14)
            act.wait_ge(lam_ps, 1)
            act_fn(st[:, 2:4], bank[:, 4, 0:2], ACT.Exp).then_inc(lam_e, 1)
            units(14, 18)
            for u in range(HEADS):
                act.wait_ge(cv_y, u + 5)
                act_fn(sgk[:, u, :], bk[:, u, :], ACT.Sigmoid).then_inc(cv_s, 1)
            units(22, 26)
            exps(0)
            for u in range(16):
                act.wait_ge(at_ps, u + 1)
                if u >= 2:
                    act.wait_ge(pv_ps, u - 1)
                act_fn(aT[:, u % 2, :], bank[:, 6, :], ACT.Copy).then_inc(at_out, 1)
                if u < 15:
                    exps(u + 1)
                if u % 4 == 3:
                    act.wait_ge(pv_ps, u + 1)
                    act_fn(og[:, u // 4, :], bank[:, 7, :], ACT.Copy).then_inc(o_out, 1)
            act.wait_ge(hn_ms, 1)
            act_fn(st[:, 104:120], st[:, 104:120], ACT.Sqrt).then_inc(hn_sd, 1)
            for t in range(TT):
                for g in range(2):
                    act.wait_ge(cT_ps, 2 * t + g + 1)
                    act_fn(hl[:, 4 * g:4 * g + 4, t * P:(t + 1) * P], bank[:, 6 + g, :].rearrange("p (k n) -> p k n", k=4),
                           ACT.Copy).then_inc(cT_out, 1)
            after_mixer(0)
            moe(0)
            for u in range(16):
                if u == 5:
                    for t in range(TT):
                        root(3, t)
                act.wait_ge(kf_ps, u + 1)
                act_fn(kf[:, u % 4, (u // 4) * NB:(u // 4 + 1) * NB], bank[:, 4 + u % 2, :], ACT.Copy).then_inc(kf_out, 1)
            for t in range(TT):
                features(3, t)
            for i in range(2):
                for q in range(4):
                    n, t = q // 2, q % 2
                    act.wait_ge(vt_ps, 4 * i + q + 1)
                    act_fn(ztok[:, t, n * NB:(n + 1) * NB], bank[:, turn_bank(i, n, t), :], ACT.Copy).then_inc(vt_out, 1)
            after_mixer(1)
            moe(1)

        @block.vector
        def _(dve):
            steps = [0]
            v = nc.vector

            def step(ins):
                steps[0] += 1
                ins.then_inc(dve_step, 1)
                dve.wait_ge(dve_step, steps[0])

            def mod_chunk(n):
                dve.wait_ge(mod_ps, n + 1)
                dve.wait_ge(s_bn[n % 2], rows_in(n))
                if n >= 6:
                    dve.wait_ge(s_mr[n % 2], stored(n - 2))
                elif n >= 2:
                    dve.wait_ge(pick_ps, 2 * (n - 1))
                m, o, bias, gain = n % 12 // 2, mr[:, n % 2, :], mod_rows(n)[:, 0, :], mod_rows(n)[:, 1, :]
                ins = v.tensor_tensor(o, bank[:, mod_bank(n), 0:P], bias, ALU.add)
                if m in (1, 4):
                    step(ins)
                    ins = v.scalar_tensor_tensor(o, o, 1.0, gain, ALU.add, ALU.mult)
                elif m in (2, 5):
                    step(ins)
                    ins = v.tensor_tensor(o, o, gain, ALU.mult)
                ins.then_inc(mod_out, 1)

            def norm_mean(i, t):
                src = (cx if i == 0 else x)[:, t, :]
                s = norm_col(i, t)
                if i > 1:
                    dve.wait_ge(hT_ps, 2 * (2 * (i - 1) + t + 1))
                squares = mod[:, 2 + t, :] if i == 1 else hh[:, t, :]
                step(v.tensor_tensor_reduce(squares, src, src, 1.0, 0.0, ALU.mult, ALU.add, st[:, s:s + 1]))
                v.tensor_scalar(st[:, s + 1:s + 2], st[:, s:s + 1], 1.0 / D, EPS, ALU.mult, ALU.add).then_inc(nrm_ms, 1)

            def norm(i, t):
                src = (cx if i == 0 else x)[:, t, :]
                table = modc if i == 0 else mod
                m = 3 if i in (2, 4) else 0
                s = norm_col(i, t)
                if i == 1:
                    dve.wait_ge(hT_ps, 2 * (t + 1))
                dve.wait_ge(nrm_sd, 2 * i + t + 1)
                step(v.reciprocal(st[:, s + 3:s + 4], st[:, s + 2:s + 3]))
                step(v.scalar_tensor_tensor(hh[:, t, :], src, st[:, s + 3:s + 4], table[:, m + 1, :], ALU.mult, ALU.mult))
                v.tensor_tensor(hh[:, t, :], hh[:, t, :], table[:, m, :], ALU.add).then_inc(nrm_h, 1)

            def post_norm(j, t):
                l, m = j // 2, 5 if j % 2 else 2
                dve.wait_ge(mix_sq, 4 * j + 2 * t + 2)
                step(v.tensor_tensor(st[:, 84 + t:85 + t], st[:, 80 + 2 * t:81 + 2 * t], st[:, 81 + 2 * t:82 + 2 * t], ALU.add))
                v.tensor_scalar(st[:, 86 + t:87 + t], st[:, 84 + t:85 + t], 1.0 / D, EPS, ALU.mult, ALU.add).then_inc(mix_ms, 1)
                dve.wait_ge(mix_sd, 2 * j + t + 1)
                step(v.reciprocal(st[:, 90 + t:91 + t], st[:, 88 + t:89 + t]))
                for n in range(HALVES):
                    half = slice(n * NB, (n + 1) * NB)
                    ins = v.scalar_tensor_tensor(hh[:, t, half], bank[:, 2 * t + n, :], st[:, 90 + t:91 + t], mod[:, m, half],
                                                 ALU.mult, ALU.mult)
                step(ins)
                v.tensor_tensor(x[:, t, :], x[:, t, :], hh[:, t, :], ALU.add).then_inc(x_out, 1)
                dve.wait_ge(x_out, 2 * j + t + 1)

            def taps(o, src, w, b, segs):
                step(v.tensor_scalar(o, src, w[1], b, ALU.mult, ALU.add))
                for s0, s1 in segs:
                    step(v.scalar_tensor_tensor(o[:, s0 + 1:s1], src[:, s0:s1 - 1], w[0], o[:, s0 + 1:s1], ALU.mult, ALU.add))
                for s0, s1 in segs:
                    ins = v.scalar_tensor_tensor(o[:, s0:s1 - 1], src[:, s0 + 1:s1], w[2], o[:, s0:s1 - 1], ALU.mult, ALU.add)
                    if (s0, s1) != segs[-1]:
                        step(ins)
                return ins

            def pcol(c):
                return par[:, c:c + 1]

            def conv_ab(u, o):
                dve.wait_ge(proj_ps, (u + 5) if u < 4 else (u + 15))
                unit = u + 4 if u < 4 else u + 14
                segs = [(0, T)] if u < 4 else [(0, T), (T, 2 * T)]
                w = [pcol(Q_CAW + 8 * j + u) for j in range(3)]
                taps(o, bank[:, unit % 4, 0:segs[-1][1]], w, pcol(Q_CAB + u), segs).then_inc(cv_y, 1)

            def conv_gate(u, o, s):
                dve.wait_ge(cv_s, u + 1)
                v.scalar_tensor_tensor(o, o, DV ** -0.5 if u < 4 else 1.0, s, ALU.mult, ALU.mult).then_inc(cv_out, 1)

            def decay_rows():
                dve.wait_ge(gate_l, 2)
                step(v.scalar_tensor_tensor(lf, fg, 0.0, lf, ALU.min, ALU.subtract))
                for s in range(2):
                    seg = slice(s * T, (s + 1) * T)
                    step(v.tensor_tensor_scan(pre[:, seg], small[0:64, C_ONES:C_ONES + T], lf[:, seg], 0.0, ALU.mult, ALU.add))
                ctx_, lat = slice(0, T), slice(T, 2 * T)
                fw, bw = slice(0, 32), slice(32, 64)
                tc, tl = pre[:, T - 1:T], pre[:, 2 * T - 1:2 * T]
                step(v.scalar_tensor_tensor(decay_c[fw, :], pre[fw, :], -1.0, ig[fw, :], ALU.mult, ALU.add))
                step(v.tensor_scalar(decay_c[fw, ctx_], decay_c[fw, ctx_], tc[fw], None, ALU.add))
                step(v.tensor_copy(decay_b[fw, :], pre[fw, lat]))
                step(v.tensor_tensor(fg[bw, :], pre[bw, :], lf[bw, :], ALU.subtract))
                step(v.tensor_tensor(decay_c[bw, :], ig[bw, :], fg[bw, :], ALU.add))
                step(v.tensor_scalar(decay_c[bw, lat], decay_c[bw, lat], tl[bw], None, ALU.subtract))
                step(v.tensor_scalar(decay_b[bw, :], fg[bw, lat], -1.0, tl[bw], ALU.mult, ALU.add))
                v.tensor_scalar(st[0:64, 8:16], small[0:64, C_ROW8:C_ROW8 + 8], tc, None, ALU.mult).then_inc(crow, 1)

            def ropes(first_q):
                dve.wait_ge(s_zero, 1)
                for q in range(first_q, first_q + 2):
                    rope_heads(q)

            def rope_heads(q):
                dve.wait_ge(rot_ps, q + 1)
                hs = slice(2 * (q % 2), 2 * (q % 2) + 2)
                src = qraw[:, hs, :] if q < 2 else kk[:, hs, T:2 * T]
                two = [P, 2, T]
                step(v.tensor_tensor(rope, bank[:, 4 + q % 2, :].rearrange("p (j t) -> p j t", j=2), sin.unsqueeze(1).broadcast_to(two), ALU.mult))
                step(v.tensor_tensor(src, src, cos.unsqueeze(1).broadcast_to(two), ALU.mult))
                if q < 2:
                    step(v.tensor_tensor(qz[0:64, 0, hs, :], src[0:64], rope[0:64], ALU.add))
                    v.tensor_tensor(qz[64:128, 1, hs, :], src[64:128], rope[64:128], ALU.add).then_inc(rot_out, 1)
                else:
                    v.tensor_tensor(src, src, rope, ALU.add).then_inc(rot_out, 1)
                dve.wait_ge(rot_out, q + 1)

            def lambda_and_decay():
                dve.wait_ge(lam_e, 1)
                step(v.tensor_tensor(st[:, 4:5], st[:, 3:4], st[:, 2:3], ALU.subtract))
                step(v.tensor_scalar(st[:, 5:6], st[:, 4:5], LAM_INIT, None, ALU.subtract))
                dve.wait_ge(bcol_ps, 1)
                step(v.tensor_copy(st[:, 16:24], bank[:, 5, 0:8]))
                for t in range(TT):
                    ins = v.tensor_copy(st[:, 24 + 8 * t:32 + 8 * t].rearrange("p (d h) -> p d h", d=2),
                                        bank[:, 5, (1 + t) * P:(1 + t) * P + 64].rearrange("p (d r) -> p d r", d=2)[:, :, 0:4])
                    if t == 0:
                        step(ins)
                ins.then_inc(bcol_out, 1)
                dve.wait_ge(bcol_out, 1)

            def stats(u):
                s = 40 + 16 * (u % 2)
                return [st[:, s + 2 * i:s + 2 * i + 2] for i in range(8)]

            def maxima(u):
                g, h, b = u // 4, u % 4, 3 * (u % 2)
                mx, neg, nmt = stats(u)[0:3]
                dve.wait_ge(score_ps, u + 1)
                if g < 2:
                    for c in range(2):
                        step(v.tensor_reduce(mx[:, c:c + 1], bank[:, b + c, :], AX_X, ALU.max))
                    v.tensor_scalar(neg, mx, -DQK ** -0.5, None, ALU.mult).then_inc(m_ready, 1)
                else:
                    if u == 8:
                        dve.wait_ge(s_ab, 64)
                    for d in range(2):
                        step(v.tensor_tensor_reduce(ex[:, u % 2, d, :], bank[:, b + 1 + d, :], mask[:, d, g % 2, :], 1.0,
                                                    st[:, 16 + 4 * d + h:17 + 4 * d + h], ALU.add, ALU.max, mx[:, d:d + 1]))
                    step(v.tensor_scalar(neg, mx, -1.0, None, ALU.mult))
                    bcols = st[:, 24 + 8 * (g % 2):32 + 8 * (g % 2)].rearrange("p (d h) -> p d h", d=2)[:, :, h]
                    v.tensor_tensor(nmt, neg, bcols, ALU.subtract).then_inc(m_ready, 1)

            def weights(u):
                g, b = u // 4, 3 * (u % 2)
                _, _, _, sm, en, r = stats(u)[0:6]
                e, o = ex[:, u % 2], amat[:, u % 2, :]
                dve.wait_ge(e_ready, 2 * (u + 1) if u < 8 else 16 + 3 * (u - 7))
                if g < 2:
                    step(v.reciprocal(r, sm))
                    step(v.tensor_scalar(r[:, 1:2], r[:, 1:2], st[:, 5:6], None, ALU.mult))
                else:
                    for d in range(2):
                        step(v.tensor_tensor_reduce(e[:, d, :], bank[:, b, :], e[:, d, :], 1.0, 0.0, ALU.mult, ALU.add,
                                                    sm[:, d:d + 1]))
                    step(v.scalar_tensor_tensor(sm, sm, -1.0, sm, ALU.mult, ALU.max))
                    step(v.tensor_tensor(sm, sm, en, ALU.max))
                    step(v.reciprocal(r, sm))
                if u >= 2:
                    dve.wait_ge(at_ps, u - 1)
                step(v.tensor_scalar(o, e[:, 0, :], r[:, 0:1], None, ALU.mult))
                v.scalar_tensor_tensor(o, e[:, 1, :], r[:, 1:2], o, ALU.mult, ALU.add).then_inc(a_ready, 1)

            def head_squares(g):
                dve.wait_ge(o_out, g + 1)
                o = cat[:, g % 2, (g // 2) * NB:(g // 2 + 1) * NB]
                for h in range(HEADS):
                    src = og[:, g, h * DV:(h + 1) * DV]
                    ins = v.tensor_tensor_reduce(o[:, h * DV:(h + 1) * DV], src, src, 1.0, 0.0, ALU.mult, ALU.add,
                                                 st[:, 104 + 4 * g + h:105 + 4 * g + h])
                step(ins)

            def head_norm(g):
                t = g % 2
                o = cat[:, t, (g // 2) * NB:(g // 2 + 1) * NB]
                for h in range(HEADS):
                    cols = slice(h * DV, (h + 1) * DV)
                    ins = v.scalar_tensor_tensor(o[:, cols], og[:, g, cols], st[:, 104 + 4 * g + h:105 + 4 * g + h],
                                                 hgain[:, g // 2, cols], ALU.mult, ALU.mult)
                if g >= 2:
                    step(ins)
                    ins = v.tensor_tensor(o, o, sigbo[:, t, :], ALU.mult)
                ins.then_inc(cat_out, 1)

            def sine_argument(i):
                if i == 0:
                    step(v.memset(raw3[:, 0, :], 0.0))
                arg, turns = raw3[0:HIDDEN, 1, :], raw3[0:HIDDEN, 2, :]
                whole = raw3[0:HIDDEN, 3, :].bitcast(I32)
                dve.wait_ge(f_ps, i + 1)
                step(v.tensor_scalar(arg, bank[0:HIDDEN, 6, 0:T], par[0:HIDDEN, Q_B + i:Q_B + i + 1], None, ALU.add))
                step(v.tensor_scalar(whole, arg, 1.0 / (2 * math.pi), None, ALU.mult))
                step(v.tensor_copy(turns, whole))
                high = 6.28125
                step(v.scalar_tensor_tensor(arg, turns, -high, arg, ALU.mult, ALU.add))
                step(v.scalar_tensor_tensor(arg, turns, -(2 * math.pi - high), arg, ALU.mult, ALU.add))
                v.tensor_scalar(arg, arg, 3.1415925, -3.1415925, ALU.min, ALU.max).then_inc(f_arg, 1)

            def filter_taps():
                dve.wait_ge(s_hy, 48)
                for u in range(8):
                    t, n = u // 4, u % 4
                    dve.wait_ge(ff_ps, u + 1)
                    v.tensor_tensor(filt[:, t, n * NB:(n + 1) * NB], bank[:, 5 + u % 2, :], window[:, t, (n % 2) * NB:(n % 2 + 1) * NB],
                                    ALU.mult).then_inc(ff_out, 1)

            def hyena():
                for u in range(24):
                    dve.wait_ge(up_ps, u + 1)
                    w = [pcol(Q_CHW + 24 * j + u) for j in range(3)]
                    taps(ut[:, u, :], bank[:, u % 4, 0:T], w, pcol(Q_CHB + u), [(0, T)]).then_inc(up_out, 1)
                dve.wait_ge(up_out, 24)
                tmp = [hl[:, 2 * j:2 * j + 2, :].rearrange("p k t -> p (k t)") for j in range(2)]
                for i in range(2):
                    for n in range(HALVES):
                        dve.wait_ge(sp_ps, 2 * i + n + 1)
                        if n:
                            dve.wait_ge(y_out, 2 * i + 1)
                        half = slice(n * NB, (n + 1) * NB)
                        for j in range(2):
                            re, im = bank[:, 4 * n + j, :], bank[:, 4 * n + 2 + j, :]
                            kr = kf[:, j, i * D + n * NB:i * D + (n + 1) * NB]
                            ki = kf[:, 2 + j, i * D + n * NB:i * D + (n + 1) * NB]
                            v.tensor_tensor(ys[:, j, half], re, kr, ALU.mult)
                            v.tensor_tensor(tmp[0], im, ki, ALU.mult)
                            v.tensor_tensor(ys[:, 2 + j, half], re, ki, ALU.mult)
                            step(v.tensor_tensor(tmp[1], im, kr, ALU.mult))
                            v.tensor_tensor(ys[:, j, half], ys[:, j, half], tmp[0], ALU.subtract)
                            ins = v.tensor_tensor(ys[:, 2 + j, half], ys[:, 2 + j, half], tmp[1], ALU.add)
                            if j == 0:
                                step(ins)
                        ins.then_inc(y_out, 1)
                    for c in range(8):
                        dve.wait_ge(iv_ps, 8 * i + c + 1)
                        step(v.scalar_tensor_tensor(ut[:, c, :], ut[:, c, :], pcol(Q_FB + 8 * i + c), bank[:, c, 0:T],
                                                    ALU.mult, ALU.add))
                        v.tensor_tensor(ut[:, c, :], ut[:, c, :], ut[:, 8 * (i + 1) + c, :], ALU.mult).then_inc(z_out, 1)
                    dve.wait_ge(z_out, 8 * (i + 1))

            def split(l):
                dve.wait_ge(hT_ps, 4 * (3 if l == 0 else 5))
                for q in range(2):
                    step(v.tensor_copy(th[:, q, 1, :], hh[:, 1, :]))
                    step(v.tensor_tensor(hh[:, 1, :], hh[:, 1, :], th[:, q, 1, :], ALU.subtract))
                v.tensor_copy(th[:, 2, 1, :], hh[:, 1, :]).then_inc(split_out, 1)

            def shared(l, t):
                dve.wait_ge(sh_sig, 2 * l + t + 1)
                step(v.tensor_tensor(sg2[:, t, :], sg2[:, t, :], bank[:, 4 + t, 0:F], ALU.mult))
                v.tensor_tensor(sg2[:, t, :], sg2[:, t, :], bank[:, 4 + t, F:2 * F], ALU.mult).then_inc(sh_h, 1)

            def route(l):
                v.memset(pgo[:, OVER:OVER + 4, :], 0.0)
                step(v.memset(over_tiles, 0.0))
                step(v.memset(g12[:, :, 8:12], BIG))
                dve.wait_ge(r_in, 32 * (l + 1))
                dve.wait_ge(r_sc, l + 1)
                step(v.tensor_tensor(bi, sc, rb.unsqueeze(1).broadcast_to([P, TT, E]), ALU.add))
                for t in range(TT):
                    for g in range(NG):
                        ins = v.max(m8[:, t, g, :], bi[:, t, 8 * g:8 * g + 8])
                step(ins)
                step(v.tensor_tensor(g12[:, :, 0:8], m8[:, :, :, 0], m8[:, :, :, 1], ALU.add))
                for t in range(TT):
                    step(v.max(top[:, t, :], g12[:, t, :]))
                    step(v.match_replace(g12r[:, t, :], top[:, t, :], g12[:, t, :], -BIG))
                step(v.tensor_tensor(gm, g12r[:, :, 0:8], g12[:, :, 0:8], ALU.not_equal))
                step(v.tensor_scalar(gm, gm, 1.0, BIG, ALU.subtract, ALU.mult))
                step(v.tensor_tensor(bi.rearrange("p t (g e) -> p (t g) e", g=NG), bi.rearrange("p t (g e) -> p (t g) e", g=NG),
                                     gm.rearrange("p t g -> p (t g)").unsqueeze(2).broadcast_to([P, TT * NG, 8]), ALU.add))
                for t in range(TT):
                    step(v.max(top[:, t, :], bi[:, t, :]))
                    step(v.match_replace(mk[:, t, :], top[:, t, :], bi[:, t, :], -3e38))
                v.tensor_tensor(mk, mk, bi, ALU.not_equal).then_inc(r_mk, 1)
                dve.wait_ge(r_mk, l + 1)

            def route_slots(l):
                step(v.tensor_tensor(sc, sc, mk, ALU.mult))
                step(v.tensor_reduce(nx[:, 2:4], sc, AX_X, ALU.add))
                step(v.reciprocal(nx[:, 2:4], nx[:, 2:4]))
                step(v.tensor_scalar(nx[:, 2:4], nx[:, 2:4], 2.5, None, ALU.mult))
                for t in range(TT):
                    v.tensor_scalar(pg[:, 0:E, 2 + t], sc[:, t, :], nx[:, 2 + t:3 + t], None, ALU.mult)
                dve.wait_ge(r_cu, l + 1)
                for t in range(TT):
                    ins = v.tensor_tensor(pg[:, 0:E, t], bank[:, 6, 128 + t * E:128 + (t + 1) * E], mk[:, t, :], ALU.mult)
                ins.then_inc(r_pg, 1)
                cnt = bank[0:E, 6, 256:257]
                step(v.tensor_scalar(nx[0:E, 0:1], cnt, float(C), None, ALU.is_gt))
                for q in (2, 3):
                    step(v.tensor_scalar(nx[0:E, 1:2], cnt, float(q * C), None, ALU.is_gt))
                    ins = v.tensor_tensor(nx[0:E, 0:1], nx[0:E, 0:1], nx[0:E, 1:2], ALU.add)
                    if q == 2:
                        step(ins)
                ins.then_inc(r_nx, 1)

            def route_over(l):
                dve.wait_ge(r_of, l + 1)
                end, total = bank[0:E, 6, 258:259], bank[0:1, 6, 260:261]
                step(v.tensor_tensor(nx[0:E, 1:2], end, nx[0:E, 0:1], ALU.subtract))
                kcol = small[0:E, C_K:C_K + OVER]
                step(v.tensor_scalar(sel[0:E, 1, :], kcol, end, None, ALU.is_ge))
                step(v.tensor_scalar(sel[0:E, 0, :], kcol, nx[0:E, 1:2], None, ALU.is_ge))
                step(v.tensor_tensor(sel[0:E, 0, :], sel[0:E, 0, :], sel[0:E, 1, :], ALU.subtract))
                step(v.tensor_scalar(sel[0:E, 1, :], kcol, nx[0:E, 1:2], 1.0, ALU.subtract, ALU.add))
                step(v.scalar_tensor_tensor(sel[0:E, 1, :], sel[0:E, 1, :], -float(C), sel[0:E, 0, :], ALU.mult, ALU.mult))
                step(v.tensor_scalar(nx[0:1, 1:2], total, 0.5, 0.25, ALU.mult, ALU.add))
                v.tensor_scalar(nx[0:1, 1:2], nx[0:1, 1:2], 1.0, None, ALU.max).then_inc(r_sel, 1)
                dve.wait_ge(r_sel, l + 1)
                dve.wait_ge(r_ov, l + 1)
                for j in range(4):
                    v.tensor_copy(pgo[:, 0:OVER, j], bank[:, 6, j * OVER:(j + 1) * OVER])
                step(v.memset(eid, 0))
                v.tensor_copy(eid[0:1, 36:37], nx[0:1, 1:2])
                v.tensor_copy(eid[0:1, 0:OVER], bank[0:1, 6, 4 * OVER:5 * OVER]).then_inc(r_id, 1)

            def build_slots(table, p, ph, gb):
                v.tensor_copy(pgc[:, :, :].rearrange("p j c -> p (j c)"),
                              table[:, bass.ds(2 * p, 2), :].rearrange("p j c -> p (j c)")).then_inc(ph.step, 1)
                dve.wait_ge(ph.step, p + (gb + 1))
                for t in range(TT):
                    v.tensor_tensor(ptb[:, t, :].rearrange("p (j s) -> p j s", j=2), const(C_SLOT, C).unsqueeze(1).broadcast_to([P, 2, C]),
                                    pgc[:, :, t:t + 1].broadcast_to([P, 2, C]), ALU.is_equal)
                for t in range(TT):
                    for j in range(2):
                        last = v.tensor_scalar(ptg[:, t, C * j:C * (j + 1)], const(C_SLOT, C), pgc[:, j, t:t + 1],
                                               pgc[:, j, 2 + t:3 + t], ALU.is_equal, ALU.mult)
                last.then_inc(ph.built, 1)

            def pair(ph, p, nb, gb, c, table):
                dve.wait_ge(ph.g_ps, 2 * p + (2 * gb + 2))
                dve.wait_ge(ph.pT_ps, p + (gb + 1))
                build_slots(table, p + 1, ph, gb)
                dve.wait_ge(ph.gu_ps, p + (nb + 1 + c))
                dve.wait_ge(ph.sig, p + (nb + 1))
                v.tensor_tensor(he, sg, bank[:, 5, 0:F], ALU.mult).then_inc(ph.hs, 1)
                dve.wait_ge(ph.hs, p + (nb + 1))
                v.tensor_tensor(he, he, bank[:, 5, F:2 * F], ALU.mult).then_inc(ph.h, 1)
                for n, o in enumerate((5, 6)):
                    dve.wait_ge(ph.y_ps, 2 * p + (2 * nb + n + 1 + 2 * c))
                    v.tensor_copy(ye[:, n, :], bank[:, o, :]).then_inc(ph.y_out, 1)

            def moe(l):
                gb = (PAIRS + 1) * l
                split(l)
                route(l)
                shared(l, 0)
                route_slots(l)
                dve.wait_ge(r_pg, l + 1)
                build_slots(pg, 0, first, gb)
                shared(l, 1)
                route_over(l)
                dve.wait_ge(r_id, l + 1)
                n = dve.value_load(eid[0:1, 36:37], min_val=1, max_val=OVER // 2)
                for p in range(2):
                    pair(first, p, PAIRS * l, gb, 0, pg)
                    if l == 0:
                        sine_argument(p)
                with dve.Fori(1, PAIRS // 2) as i:
                    for b in range(2):
                        pair(first, 2 * i + b, PAIRS * l, gb, 0, pg)
                with dve.Fori(0, n) as i:
                    pair(further[l], i, 0, 0, 1, pgo)
                if l == 0:
                    filter_taps()
                for t in range(TT):
                    post_norm(2 * l + 1, t)

            step(v.memset(st[:, :], 0.0))
            dve.wait_ge(s_silu, 1)
            step(v.tensor_tensor(st[:, 64:80], st[:, 64:80], par[:, Q_C:Q_C + 16], ALU.mult))
            for r in range(2):
                v.tensor_copy(cs[:, :, 16 * r:16 * (r + 1)],
                              st[:, 64 + 8 * r:72 + 8 * r].unsqueeze(2).broadcast_to([P, KT, 16])).then_inc(s_cbc, 1)
            dve.wait_ge(s_wg, 16)
            step(v.memset(wgz, 0.0))
            for f in range(2):
                for d in range(2):
                    ins = v.tensor_copy(wgz[:, :, f, 32 * d:32 * d + 4], wgr[:, :, 8 * d + 4 * f:8 * d + 4 * f + 4])
            ins.then_inc(gate_w, 1)
            step(v.memset(bnf, 0.0))
            for n in range(4):
                mod_chunk(n)
            for i, arrived in enumerate((s_tok, s_lat)):
                dve.wait_ge(arrived, 16)
                for t in range(TT):
                    norm_mean(i, t)
                if i == 0:
                    dve.wait_ge(pick_out, 8)
                for t in range(TT):
                    norm(i, t)
            dve.wait_ge(gate_ps, 2)
            step(v.tensor_scalar(ig, bank[0:64, 4, :], par[0:64, Q_GB:Q_GB + 1], None, ALU.add))
            step(v.tensor_scalar(fg, bank[64:128, 4, :], par[64:128, Q_GB:Q_GB + 1], None, ALU.add))
            v.scalar_tensor_tensor(lf, fg, -1.0, fg, ALU.mult, ALU.min).then_inc(gate_x, 1)
            decay_rows()
            lv = par[:, Q_LV:Q_LV + 4].rearrange("p (a b) -> p a b", a=2)
            v.tensor_tensor(st[:, 0:2], lv[:, :, 0], lv[:, :, 1], ALU.mult).then_inc(lam_p, 1)
            for n in range(4, 6):
                mod_chunk(n)
            for u in range(HEADS):
                conv_ab(u, bq[:, u, :])
            for u in range(HEADS):
                conv_gate(u, bq[:, u, :], sgq[:, u, :])
            for n in range(6, 12):
                mod_chunk(n)
            lambda_and_decay()
            ropes(0)
            for n in range(12, 14):
                mod_chunk(n)
            for u in range(HEADS):
                conv_ab(4 + u, bk[:, u, :])
            ropes(2)
            for u in range(HEADS):
                conv_gate(4 + u, bk[:, u, :], sgk[:, u, :])
            for n in range(14, MOD_AB):
                mod_chunk(n)
            dve.wait_ge(cv_out, 8)
            maxima(0)
            step(v.tensor_scalar(hgain[:, 0, :], hgain[:, 0, :], 1.0 - LAM_INIT, None, ALU.mult))
            for u in range(16):
                weights(u)
                if 1 <= u <= 24 - MOD_AB:
                    mod_chunk(MOD_AB - 1 + u)
                if u < 15:
                    maxima(u + 1)
                if u in (5, 9, 13):
                    head_squares(u // 4 - 1)
            head_squares(3)
            v.tensor_scalar(st[:, 104:120], st[:, 104:120], 1.0 / DV, EPS, ALU.mult, ALU.add).then_inc(hn_ms, 1)
            dve.wait_ge(hn_sd, 1)
            step(v.reciprocal(st[:, 104:120], st[:, 104:120]))
            for g in (0, 2, 1, 3):
                head_norm(g)
            dve.wait_ge(s_mod, 16)
            for t in range(TT):
                post_norm(0, t)
                norm_mean(2, t)
                norm(2, t)
            moe(0)
            for t in range(TT):
                norm_mean(3, t)
            dve.wait_ge(s_mod, 32)
            for t in range(TT):
                norm(3, t)
            hyena()
            dve.wait_ge(s_mod, 48)
            for t in range(TT):
                post_norm(2, t)
                norm_mean(4, t)
                norm(4, t)
            moe(1)


def _columns(a):
    return a.reshape(-1, P).T


def _rows(a):
    out = np.zeros((P,) + a.shape[1:], a.dtype)
    out[:a.shape[0]] = a
    return out


_LARGE = ["x", "ctx", "w_mod", "w_in_ab", "head_g_a", "head_g_b", "w_out_ab", "w_in_hy",
          "w_out_hy", "router_w", "router_b", "exp_gu", "exp_down", "sh_gu", "sh_down"]


def kernel(**inputs):
    import concourse.bacc as _bacc
    from concourse.bass_utils import run_bass_kernel_spmd as _run

    a = {k: np.asarray(v) for k, v in inputs.items()}
    arrays = {name: np.ascontiguousarray(a[name]) for name in _LARGE}
    gates = np.zeros((2, P // 2, 1), np.float32)
    gb = a["gate_b_ab"][0].reshape(2, 2, HEADS)
    for d in range(2):
        gates[:, 32 * d:32 * d + HEADS, 0] = gb[d]
    cols = [_columns(a["c"][0]), _columns(a["c_ctx"])]
    cols += [np.concatenate([_columns(a["conv_ab_w"][0, j]) for j in range(3)], 1), _columns(a["conv_ab_b"][0])]
    cols += [np.concatenate([_columns(a["conv_hy_w"][0, j]) for j in range(3)], 1), _columns(a["conv_hy_b"][0])]
    cols += [_columns(a["filt_bias"][0].reshape(-1)), gates.reshape(P, 1), _rows(a["diff_lambda"][0].T)]
    cols += [_rows(a["filt_w1"][0]), _rows(a["filt_w2"][0]), _rows(a["filt_b1"][0][:, None]),
             _rows(a["filt_b2"][0][:, None])]
    arrays["params"] = np.ascontiguousarray(np.concatenate(cols, 1))
    rows = np.zeros((24, 4, 2, P), np.float32)
    for n in range(24):
        m, cols = n % 12 // 2, slice(n % 2 * NB, (n % 2 + 1) * NB)
        rows[n, :, 0] = a["b_mod"][n // 12, n % 12 * NB:(n % 12 + 1) * NB].reshape(4, P)
        if m in (1, 2, 4, 5):
            rows[n, :, 1] = a["norm_g"][n // 12, (1, 2, 4, 5).index(m), cols].reshape(4, P)
    arrays["mod_rows"] = np.repeat(rows, 32, 1)
    arrays["filt_w3"] = _rows(a["filt_w3"][0])
    arrays.update(shape_constants())
    nc = _bacc.Bacc("TRN2", target_bir_lowering=False, num_devices=1)
    args = {n: nc.dram_tensor(f"in_{n}", v.shape, mybir.dt.from_np(v.dtype), kind="ExternalInput").ap()
            for n, v in arrays.items()}
    out = nc.dram_tensor("out_dram", (1, T, D), F32, kind="ExternalOutput").ap()
    build(nc, args, out)
    r = _run(nc, [{f"in_{n}": v for n, v in arrays.items()}], core_ids=[0])
    return r.results[0]["out_dram"]
```
